# Optimizing a Trainium2 kernel written in Bass

```python
import jax, jax.numpy as jnp
from jax import lax
import numpy as np
import math

D_MODEL = 1024
BATCH = 1
SEQ = 256
DEPTH = 1

MEM_LEN = 256
EXPAND = 2
D_MIX = EXPAND * D_MODEL
GLA_HEADS = 4
GLA_HEAD_K = 128
GLA_HEAD_V = 256
GLA_KEY_WIDTH = GLA_HEADS * GLA_HEAD_K
GLA_VAL_WIDTH = GLA_HEADS * GLA_HEAD_V
GLA_LOWRANK = 16
GLA_GATE_TAU = 16.0
HGRN_HEADS = 4
HGRN_HEAD_DIM = 128
HGRN_WIDTH = HGRN_HEADS * HGRN_HEAD_DIM
LB_FLOOR = 1e-30
XATTN_HEADS = 4
XATTN_HEAD_DIM = 128
XATTN_WIDTH = XATTN_HEADS * XATTN_HEAD_DIM
SPLIT_SIZES = (GLA_KEY_WIDTH, GLA_KEY_WIDTH, GLA_VAL_WIDTH, GLA_LOWRANK,
               HGRN_WIDTH, HGRN_WIDTH, HGRN_WIDTH,
               XATTN_WIDTH,
               D_MIX)
D_IN_PROJ = 6160
CHUNK = 16
NORM_EPS = 1e-6


def rms_norm(x, w):
    xf = x.astype(jnp.float32)
    y = xf * lax.rsqrt(jnp.mean(xf * xf, axis=-1, keepdims=True) + NORM_EPS)
    return (y * w.astype(jnp.float32)).astype(x.dtype)

def split_heads(t, n_heads):
    b, s, w = t.shape
    return t.reshape(b, s, n_heads, w // n_heads).transpose(0, 2, 1, 3)

def merge_heads(t):
    b, h, s, d = t.shape
    return t.transpose(0, 2, 1, 3).reshape(b, s, h * d)

def chunked_gated_linear_attention(q, k, v, log_g):
    b_, h_, s_, dk = q.shape
    dv = v.shape[-1]
    n = s_ // CHUNK
    qf = q.astype(jnp.float32).reshape(b_, h_, n, CHUNK, dk)
    kf = k.astype(jnp.float32).reshape(b_, h_, n, CHUNK, dk)
    vf = v.astype(jnp.float32).reshape(b_, h_, n, CHUNK, dv)
    bcum = jnp.cumsum(log_g.astype(jnp.float32).reshape(b_, h_, n, CHUNK, dk), axis=3)
    b_last = bcum[..., CHUNK - 1:CHUNK, :]
    causal = jnp.tril(jnp.ones((CHUNK, CHUNK), dtype=bool))[:, :, None]
    diff = bcum[..., :, None, :] - bcum[..., None, :, :]
    decay = jnp.where(causal, jnp.exp(jnp.where(causal, diff, 0.0)), 0.0)
    scores = jnp.einsum('bhnid,bhnjd,bhnijd->bhnij', qf, kf, decay)
    o_intra = jnp.einsum('bhnij,bhnjv->bhniv', scores, vf)
    chunk_kv = jnp.einsum('bhncd,bhncv->bhndv', kf * jnp.exp(b_last - bcum), vf)
    chunk_decay = jnp.exp(b_last[..., 0, :])

    def step(state, inp):
        dec, kv = inp
        return dec[..., None] * state + kv, state

    init = jnp.zeros((b_, h_, dk, dv), jnp.float32)
    _, states_prev = lax.scan(step, init, (jnp.moveaxis(chunk_decay, 2, 0), jnp.moveaxis(chunk_kv, 2, 0)))
    o_inter = jnp.einsum('bhncd,nbhdv->bhncv', qf * jnp.exp(bcum), states_prev)
    return (o_intra + o_inter).reshape(b_, h_, s_, dv)

def first_inputs(seed: int = 0) -> dict:
    key = jax.random.key(seed)
    ks = jax.random.split(key, 14)
    f32 = jnp.float32
    nrm = lambda k, shape, scale: (jax.random.normal(k, shape, f32) * scale).astype(f32)
    return {
        "x": nrm(ks[0], (BATCH, SEQ, D_MODEL), 1.0),
        "mem": nrm(ks[1], (BATCH, MEM_LEN, D_MODEL), 1.0),
        "norm_w": 1.0 + nrm(ks[2], (DEPTH, D_MODEL), 0.1),
        "w_in": nrm(ks[3], (DEPTH, D_MODEL, D_IN_PROJ), D_MODEL ** -0.5),
        "gla_w_gate_up": nrm(ks[4], (DEPTH, GLA_LOWRANK, GLA_KEY_WIDTH), GLA_LOWRANK ** -0.5),
        "gla_b_gate": nrm(ks[5], (DEPTH, GLA_KEY_WIDTH), 0.1),
        "gla_norm_w": 1.0 + nrm(ks[6], (DEPTH, GLA_HEAD_V), 0.1),
        "hgrn_lower_bounds": nrm(ks[7], (DEPTH, HGRN_WIDTH), 0.5),
        "hgrn_norm_w": 1.0 + nrm(ks[8], (DEPTH, HGRN_HEAD_DIM), 0.1),
        "mem_norm_w": 1.0 + nrm(ks[9], (DEPTH, D_MODEL), 0.1),
        "w_mem_kv": nrm(ks[10], (DEPTH, D_MODEL, 2 * XATTN_WIDTH), D_MODEL ** -0.5),
        "xattn_norm_w": 1.0 + nrm(ks[11], (DEPTH, XATTN_HEAD_DIM), 0.1),
        "w_out": nrm(ks[12], (DEPTH, D_MIX, D_MODEL), D_MIX ** -0.5),
        "final_norm_w": 1.0 + nrm(ks[13], (D_MODEL,), 0.1),
    }

def first_block(x, mem, norm_w, w_in, gla_w_gate_up, gla_b_gate, gla_norm_w, hgrn_lower_bounds,
              hgrn_norm_w, mem_norm_w, w_mem_kv, xattn_norm_w, w_out, final_norm_w):
    dtype = x.dtype
    split_idx = [int(i) for i in np.cumsum(SPLIT_SIZES)[:-1]]
    lb_p = jax.nn.softmax(hgrn_lower_bounds.astype(jnp.float32), axis=0)
    lower_bounds = jnp.cumsum(lb_p, axis=0) - lb_p[0]

    for layer in range(DEPTH):
        h = rms_norm(x, norm_w[layer])
        proj = jnp.einsum('bsd,de->bse', h, w_in[layer])
        (gq, gk, gv, glr, hq, hf, hi, xq, gate) = jnp.split(proj, split_idx, axis=-1)

        glr_up = jnp.einsum('bsr,rk->bsk', glr, gla_w_gate_up[layer]) + gla_b_gate[layer]
        gla_log_a = jax.nn.log_sigmoid(glr_up.astype(jnp.float32)) / GLA_GATE_TAU
        gla_o = chunked_gated_linear_attention(
            split_heads(gq, GLA_HEADS) * (GLA_HEAD_K ** -0.5), split_heads(gk, GLA_HEADS),
            split_heads(gv, GLA_HEADS), split_heads(gla_log_a, GLA_HEADS))
        gla_o = merge_heads(rms_norm(gla_o, gla_norm_w[layer]))

        lb = lower_bounds[layer]
        zf = hf.astype(jnp.float32)
        hgrn_log_f = jnp.logaddexp(jnp.log(jnp.maximum(lb, LB_FLOOR)),
                                   jnp.log1p(-lb) + jax.nn.log_sigmoid(zf))
        hgrn_k = (1.0 - lb) * jax.nn.sigmoid(-zf)
        hgrn_o = chunked_gated_linear_attention(
            split_heads(hq, HGRN_HEADS), split_heads(hgrn_k, HGRN_HEADS),
            split_heads(hi, HGRN_HEADS), split_heads(hgrn_log_f, HGRN_HEADS))
        hgrn_o = merge_heads(rms_norm(hgrn_o, hgrn_norm_w[layer]))

        m = rms_norm(mem, mem_norm_w[layer])
        mkv = jnp.einsum('bmd,de->bme', m, w_mem_kv[layer])
        mk, mv = jnp.split(mkv, 2, axis=-1)
        s = jnp.einsum('bhsd,bhmd->bhsm', split_heads(xq, XATTN_HEADS).astype(jnp.float32),
                       split_heads(mk, XATTN_HEADS).astype(jnp.float32)) * (XATTN_HEAD_DIM ** -0.5)
        p = jax.nn.softmax(s, axis=-1)
        xo = jnp.einsum('bhsm,bhmd->bhsd', p, split_heads(mv, XATTN_HEADS).astype(jnp.float32))
        xo = merge_heads(rms_norm(xo, xattn_norm_w[layer]))

        mixed = jnp.concatenate([gla_o, hgrn_o, xo], axis=-1).astype(dtype)
        mixed = mixed * jax.nn.silu(gate)
        x = x + jnp.einsum('bse,ed->bsd', mixed, w_out[layer]).astype(dtype)

    return rms_norm(x, final_norm_w)


N_META = 16
D_FF = 2816
EPS = 1e-6
FOURIER_GROUPS = 8
FOURIER_GROUP_DIM = 64
D_FOURIER = FOURIER_GROUPS * FOURIER_GROUP_DIM
D_SCONV = 512
SCONV_WIDTH = 3
DN_HEADS = 4
DN_HEAD_DIM = 128
D_DN = DN_HEADS * DN_HEAD_DIM
DN_CONV_WIDTH = 3
CHUNK_2 = 64
N_BRANCH = 3
PROJ_SIZES = (D_FOURIER, 3 * D_SCONV, 3 * D_DN, D_DN, 2 * DN_HEADS, 2 * DN_HEADS, N_BRANCH * D_MODEL)
D_IN_PROJ_2 = D_FOURIER + 3 * D_SCONV + 3 * D_DN + D_DN + 4 * DN_HEADS + N_BRANCH * D_MODEL


def rmsnorm(x, g):
    xf = x.astype(jnp.float32)
    y = xf * lax.rsqrt(jnp.mean(xf * xf, axis=-1, keepdims=True) + EPS)
    return (y * g.astype(jnp.float32)).astype(x.dtype)

def swiglu(x, wi, wo):
    a, b = jnp.split(x @ wi, 2, axis=-1)
    return (jax.nn.silu(a) * b) @ wo

def conv3_centred(x, w):
    xp = jnp.pad(x, ((0, 0), (1, 1), (0, 0)))
    return w[0] * xp[:, :-2] + w[1] * xp[:, 1:-1] + w[2] * xp[:, 2:]

def fourier_mix(u):
    B, L, _ = u.shape
    ug = u.astype(jnp.float32).reshape(B, L, FOURIER_GROUPS, FOURIER_GROUP_DIM)
    y = jnp.fft.fft2(ug, axes=(1, 3), norm="ortho").real
    return y.reshape(B, L, D_FOURIER).astype(u.dtype)

def short_conv_mix(u, w):
    b, c, h = jnp.split(u, 3, axis=-1)
    return b * conv3_centred(c * h, w)

def l2norm(x):
    return x * lax.rsqrt(jnp.sum(x * x, axis=-1, keepdims=True) + EPS)

def chunk_gated_delta(q, k, v, beta, g):
    B, H, N, C, DK = q.shape
    DV = v.shape[-1]
    lower = jnp.tril(jnp.ones((C, C), bool))
    strict = jnp.tril(jnp.ones((C, C), bool), -1)
    gc = jnp.cumsum(g, axis=-1)
    diff = gc[..., :, None] - gc[..., None, :]
    decay_mask = jnp.exp(jnp.where(lower, diff, -jnp.inf))
    k_beta = k * beta[..., None]
    v_beta = v * beta[..., None]
    m = jnp.where(strict, jnp.einsum('bhnck,bhnsk->bhncs', k_beta, k) * decay_mask, 0.0)
    eye = jnp.eye(C, dtype=q.dtype)
    t = lax.linalg.triangular_solve(eye + m, jnp.broadcast_to(eye, m.shape), left_side=True,
                                    lower=True, unit_diagonal=True)
    u = t @ v_beta
    w = t @ (k_beta * jnp.exp(gc)[..., None])
    attn = jnp.einsum('bhnck,bhnsk->bhncs', q, k) * decay_mask
    q_dec = q * jnp.exp(gc)[..., None]
    k_dec = k * jnp.exp(gc[..., -1:] - gc)[..., None]
    g_last = jnp.exp(gc[..., -1])

    def step(S, xs):
        attn_n, u_n, w_n, qd_n, kd_n, gl_n = xs
        v_new = u_n - w_n @ S
        o = qd_n @ S + attn_n @ v_new
        S = S * gl_n[..., None, None] + jnp.swapaxes(kd_n, -1, -2) @ v_new
        return S, o

    xs = tuple(jnp.moveaxis(a, 2, 0) for a in (attn, u, w, q_dec, k_dec, g_last))
    S0 = jnp.zeros((B, H, DK, DV), q.dtype)
    _, o = lax.scan(step, S0, xs)
    return jnp.moveaxis(o, 0, 2)

def deltanet_branch(qkv, z, beta_logit, alpha_logit, conv_w, A_log, dt_bias, norm_w):
    B, L, _ = qkv.shape
    f32 = jnp.float32
    qkv = jax.nn.silu(conv3_centred(qkv, conv_w)).astype(f32)
    q, k, v = jnp.split(qkv, 3, axis=-1)
    q = l2norm(q.reshape(B, L, DN_HEADS, DN_HEAD_DIM)) * (DN_HEAD_DIM ** -0.5)
    k = l2norm(k.reshape(B, L, DN_HEADS, DN_HEAD_DIM))
    v = v.reshape(B, L, DN_HEADS, DN_HEAD_DIM)
    beta = jax.nn.sigmoid(beta_logit.astype(f32)).reshape(B, L, 2, DN_HEADS)
    g = -jnp.exp(A_log.astype(f32)) * jax.nn.softplus(
        alpha_logit.astype(f32).reshape(B, L, 2, DN_HEADS) + dt_bias.astype(f32))
    pad = CHUNK_2 - N_META
    padt = lambda a: jnp.pad(a, ((0, 0), (pad, 0)) + ((0, 0),) * (a.ndim - 2))
    q, k, v, beta, g = padt(q), padt(k), padt(v), padt(beta), padt(g)
    Lp = L + pad
    N = Lp // CHUNK_2

    def chunks4(a):
        return a.reshape(B, N, CHUNK_2, DN_HEADS, -1).transpose(0, 3, 1, 2, 4)

    def chunks3(a):
        return a.reshape(B, N, CHUNK_2, DN_HEADS).transpose(0, 3, 1, 2)

    def unchunk(o):
        return o.transpose(0, 2, 3, 1, 4).reshape(B, Lp, DN_HEADS, DN_HEAD_DIM)

    o_fwd = unchunk(chunk_gated_delta(chunks4(q), chunks4(k), chunks4(v),
                                      chunks3(beta[:, :, 0]), chunks3(g[:, :, 0])))
    fl = lambda a: jnp.flip(a, axis=1)
    o_bwd = fl(unchunk(chunk_gated_delta(chunks4(fl(q)), chunks4(fl(k)), chunks4(fl(v)),
                                         chunks3(fl(beta[:, :, 1])), chunks3(fl(g[:, :, 1])))))
    o = (o_fwd + o_bwd)[:, pad:]
    o = o * lax.rsqrt(jnp.mean(o * o, axis=-1, keepdims=True) + EPS) * norm_w.astype(f32)
    o = o * jax.nn.silu(z.astype(f32).reshape(B, L, DN_HEADS, DN_HEAD_DIM))
    return o.reshape(B, L, D_DN).astype(z.dtype)

def hybrid_mixer(h, w_in, sconv_w, dn_conv_w, dn_A_log, dn_dt_bias, dn_norm,
                 w_fourier, w_sconv_out, w_dn_out, w_out):
    B, L, D = h.shape
    proj = h @ w_in
    idx = [int(s) for s in np.cumsum(PROJ_SIZES)[:-1]]
    u_f, u_sc, u_qkv, z, b_logit, a_logit, gate_logit = jnp.split(proj, idx, axis=-1)
    y_f = fourier_mix(u_f) @ w_fourier
    y_sc = short_conv_mix(u_sc, sconv_w) @ w_sconv_out
    y_dn = deltanet_branch(u_qkv, z, b_logit, a_logit, dn_conv_w, dn_A_log, dn_dt_bias,
                           dn_norm) @ w_dn_out
    gates = jax.nn.sigmoid(gate_logit).reshape(B, L, N_BRANCH, D)
    merged = gates[:, :, 0] * y_f + gates[:, :, 1] * y_sc + gates[:, :, 2] * y_dn
    return merged @ w_out

def second_inputs(seed: int = 0) -> dict:
    key = jax.random.key(seed)
    ks = jax.random.split(key, 20)
    f32 = jnp.float32

    def dense(k, shape, fan_in):
        return jax.random.normal(k, shape, f32) * fan_in ** -0.5

    x = jax.random.normal(ks[0], (BATCH, SEQ, D_MODEL), f32)
    meta_tokens = jax.random.normal(ks[1], (N_META, D_MODEL), f32)
    norm_gains = 1.0 + 0.05 * jax.random.normal(ks[2], (DEPTH, 6, D_MODEL), f32)
    ffn1_wi = dense(ks[3], (DEPTH, D_MODEL, 2 * D_FF), D_MODEL)
    ffn1_wo = dense(ks[4], (DEPTH, D_FF, D_MODEL), D_FF)
    ffn2_wi = dense(ks[5], (DEPTH, D_MODEL, 2 * D_FF), D_MODEL)
    ffn2_wo = dense(ks[6], (DEPTH, D_FF, D_MODEL), D_FF)
    w_in = dense(ks[7], (DEPTH, D_MODEL, D_IN_PROJ_2), D_MODEL)
    sconv_w = dense(ks[8], (DEPTH, SCONV_WIDTH, D_SCONV), SCONV_WIDTH)
    dn_conv_w = dense(ks[9], (DEPTH, DN_CONV_WIDTH, 3 * D_DN), DN_CONV_WIDTH)
    dn_A_log = jnp.log(jax.random.uniform(ks[10], (DEPTH, 2, DN_HEADS), f32, 1.0, 16.0))
    dt = jnp.exp(jax.random.uniform(ks[11], (DEPTH, 2, DN_HEADS), f32,
                                    math.log(1e-3), math.log(1e-1)))
    dn_dt_bias = dt + jnp.log(-jnp.expm1(-dt))
    dn_norm = 1.0 + 0.05 * jax.random.normal(ks[12], (DEPTH, DN_HEAD_DIM), f32)
    w_fourier = dense(ks[13], (DEPTH, D_FOURIER, D_MODEL), D_FOURIER)
    w_sconv_out = dense(ks[14], (DEPTH, D_SCONV, D_MODEL), D_SCONV)
    w_dn_out = dense(ks[15], (DEPTH, D_DN, D_MODEL), D_DN)
    w_out = dense(ks[16], (DEPTH, D_MODEL, D_MODEL), D_MODEL)
    return {"x": x, "meta_tokens": meta_tokens, "norm_gains": norm_gains,
            "ffn1_wi": ffn1_wi, "ffn1_wo": ffn1_wo, "ffn2_wi": ffn2_wi, "ffn2_wo": ffn2_wo,
            "w_in": w_in, "sconv_w": sconv_w, "dn_conv_w": dn_conv_w, "dn_A_log": dn_A_log,
            "dn_dt_bias": dn_dt_bias, "dn_norm": dn_norm, "w_fourier": w_fourier,
            "w_sconv_out": w_sconv_out, "w_dn_out": w_dn_out, "w_out": w_out}

def second_block(x, meta_tokens, norm_gains, ffn1_wi, ffn1_wo, ffn2_wi, ffn2_wo, w_in, sconv_w,
              dn_conv_w, dn_A_log, dn_dt_bias, dn_norm, w_fourier, w_sconv_out, w_dn_out, w_out):
    B = x.shape[0]
    meta = jnp.broadcast_to(meta_tokens[None].astype(x.dtype), (B, N_META, D_MODEL))
    h = jnp.concatenate([meta, x], axis=1)
    for l in range(DEPTH):
        n = norm_gains[l]
        h = h + 0.5 * rmsnorm(swiglu(rmsnorm(h, n[0]), ffn1_wi[l], ffn1_wo[l]), n[1])
        h = h + rmsnorm(hybrid_mixer(rmsnorm(h, n[2]), w_in[l], sconv_w[l], dn_conv_w[l],
                                     dn_A_log[l], dn_dt_bias[l], dn_norm[l], w_fourier[l],
                                     w_sconv_out[l], w_dn_out[l], w_out[l]), n[3])
        h = h + 0.5 * rmsnorm(swiglu(rmsnorm(h, n[4]), ffn2_wi[l], ffn2_wo[l]), n[5])
    return h[:, N_META:]


def setup_inputs(seed=0):
    out = dict(first_inputs(seed))
    for name, value in second_inputs(seed + 1).items():
        if name != "x":
            out[name + "_2"] = value
    return out


def reference(
    x, mem, norm_w, w_in, gla_w_gate_up, gla_b_gate, gla_norm_w, hgrn_lower_bounds, hgrn_norm_w,
    mem_norm_w, w_mem_kv, xattn_norm_w, w_out, final_norm_w, meta_tokens_2, norm_gains_2,
    ffn1_wi_2, ffn1_wo_2, ffn2_wi_2, ffn2_wo_2, w_in_2, sconv_w_2, dn_conv_w_2, dn_A_log_2,
    dn_dt_bias_2, dn_norm_2, w_fourier_2, w_sconv_out_2, w_dn_out_2, w_out_2,
):
    x = first_block(
        x, mem, norm_w, w_in, gla_w_gate_up, gla_b_gate, gla_norm_w, hgrn_lower_bounds,
        hgrn_norm_w, mem_norm_w, w_mem_kv, xattn_norm_w, w_out, final_norm_w,
    )
    return second_block(
        x, meta_tokens_2, norm_gains_2, ffn1_wi_2, ffn1_wo_2, ffn2_wi_2, ffn2_wo_2, w_in_2,
        sconv_w_2, dn_conv_w_2, dn_A_log_2, dn_dt_bias_2, dn_norm_2, w_fourier_2, w_sconv_out_2,
        w_dn_out_2, w_out_2,
    )


_drawn_inputs = setup_inputs


def setup_inputs(seed=0):
    import zlib

    import numpy as np

    out = dict(_drawn_inputs(seed))
    spreads = {}
    factors = {'dn_norm_2': 3.82}
    for name, (base, spread) in spreads.items():
        noise = np.random.default_rng([zlib.crc32(name.encode()), seed]).standard_normal(out[name].shape)
        drawn = base * np.exp(spread * noise) if base else spread * noise
        out[name] = __import__('jax').numpy.asarray(drawn.astype(out[name].dtype))
    for name, factor in factors.items():
        out[name] = (out[name] * factor).astype(out[name].dtype)
    return out
```

```python
import concourse.bass as bass
from concourse import mybir
from contextlib import ExitStack

P = 128
ROWS = 256
META = 16
LEN = META + ROWS
KT = 8
HEADS = 8
UP = 44
FT = 22
CH = 68
NC = LEN // CH
SUB = 17
RING = 4
LEAD = 3
EPS = 1e-6
FLOOR = 1e-30

MEM_P, IN_P, WOUT_P, UP1_P = 0, 8, 56, 72
DOWN1_P = UP1_P + UP
MIX_P = DOWN1_P + 24
OUT2_P = MIX_P + 56 + 12
UP2_P = OUT2_P + 8
DOWN2_P = UP2_P + UP
PANELS = DOWN2_P + 24
MEM_O, IN_O, WOUT_O, UP1_O = 0, 8, 56, 64
DOWN1_O = UP1_O + UP
MIX_O = DOWN1_O + 8
OUT2_O = MIX_O + 56 + 24
UP2_O = OUT2_O + 8
DOWN2_O = UP2_O + UP

VEC = {}
for _name, _width in (("norm_w", 8), ("mem_norm", 8), ("final", 8), ("gains", 48), ("b_gate", 4),
                      ("gla_norm", 2), ("lb", 4), ("hgrn_norm", 1), ("xattn_norm", 1), ("sconv", 12),
                      ("dconv", 36), ("dn_norm", 1), ("a_log", 8), ("dt_bias", 8)):
    VEC[_name] = sum(w for _, w in VEC.values()) if VEC else 0, _width
VEC_AT = {n: a for n, (a, _) in VEC.items()}
VECS = sum(w for _, w in VEC.values())


XQ, GATE, V = 16, 20, 36


def first_schedule():
    steps = [("lowrank",)]
    steps += [("out", i) for i in range(16)]
    steps += [("decay",)]
    for n in range(18):
        steps += [("level", n // 2, n % 2), ("out", XQ + n)]
    steps += [("out", XQ + 18), ("out", XQ + 19)]
    for u in (0, 2):
        steps += [("scores", u), ("scores", u + 1), ("weights", u), ("weights", u + 1)]
        steps += [("out", V + u), ("out", V + u + 1), ("probs", u), ("probs", u + 1)]
    for q in range(10):
        steps += [("out", V + 2 + 2 * q), ("out", V + 3 + 2 * q)] if 1 <= q < 5 else []
        steps += [("o", q)] if q < 8 else []
        steps += [("o_norm", q - 1)] if 1 <= q < 9 else []
        steps += [("o_split", q - 2)] if q >= 2 else []
        steps += [("wout", q - 6)] if q >= 6 else []
    return steps


def mixer_schedule():
    steps = [("qkv", 0), ("qkv", 1), ("logits",), ("qkv", 2), ("cumulate",)]
    steps += [("qkv", i) for i in range(3, 7)] + [("silu", 0)]
    steps += [("qkv", i) for i in range(7, 11)] + [("silu", 1), ("qkv", 11)]
    steps += [("z", 0), ("silu", 2), ("z", 1), ("z", 2), ("z", 3), ("l2norm",), ("fourier_in", 0), ("fourier_in", 1)]
    steps += [("chunk", 0), ("fourier_in", 2), ("chunk", 1), ("fourier_in", 3), ("chunk", 2), ("chunk", 3)]
    steps += [("gather",), ("dft", 0), ("dft", 1), ("blocks",), ("dft", 2), ("dft", 3), ("invert",)]

    def gates(b):
        for i in range(0, 8, 2):
            yield from (("gate", b, i), ("gate", b, i + 1), ("branch", b, i), ("branch", b, i + 1))

    conv = [("sconv", i, j) for i in range(4) for j in range(3)]
    panels = conv[:2] + list(gates(0)) + conv[2:] + list(gates(1))
    delta = []
    for t in range(8 + 3):
        for kind, u in (("u0", t), ("x17", t - 1), ("t17", t - 2), ("u17", t - 3)):
            delta += [(kind, u)] if 0 <= u < 8 else []
    for t in range(8 + 1):
        for kind, u in (("x34", t), ("t34", t - 1)):
            delta += [(kind, u)] if 0 <= u < 8 else []
    steps += panels[:4] + [("inverses",)] + panels[4:6] + [("scatter",)] + panels[6:9]
    panels = panels[9:]
    for n in range(24):
        steps += delta[2 * n:2 * n + 2] + panels[:1]
        panels = panels[1:]
    for c in range(NC):
        for kind in ("ks", "vn", "od", "su"):
            if (kind, c) not in (("ks", 0), ("su", NC - 1)):
                steps += [(kind, c)] + panels[:1]
                panels = panels[1:]
    steps += panels + [("delta_norm",)] + list(gates(2))
    return steps


FIRST, MIXER = first_schedule(), mixer_schedule()


def aux_uses():
    uses = [("stat", 0), ("stat", 1)]
    for step in FIRST:
        kind, rest = step[0], step[1:]
        if kind in ("lowrank", "o"):
            uses += [step]
        elif kind == "decay":
            uses += [("up", 0), ("up", 1)]
        elif kind == "level":
            uses += [step + (x,) for x in range(2 if rest[0] < 8 else 1)]
        elif kind in ("scores", "probs"):
            uses += [step]
        elif kind == "o_norm":
            uses += [step]
    uses += [("stat", n) for n in (2, 3, 4, 5)]
    for step in MIXER:
        kind, rest = step[0], step[1:]
        if kind == "logits":
            uses += [("ba",), step]
        if kind in ("cumulate", "u0", "x17", "t17", "u17", "x34", "t34"):
            uses += [step]
        elif kind == "l2norm":
            uses += [("l2", i) for i in range(8)]
        elif kind == "chunk":
            uses += [(use,) + rest for use in ("kt", "vt", "row0", "row1", "kk", "qk")]
        elif kind == "dft":
            uses += [("dft_in", rest[0], 0), ("dft_in", rest[0], 1), ("dft_out", rest[0])]
        elif kind in ("ks", "vn", "od", "su"):
            uses += [step + (d,) for d in range(2)]
        elif kind == "delta_norm":
            uses += [("dstat", i) for i in range(2)]
    uses += [("stat", n) for n in (6, 7, 8)]
    return uses


AUX = {use: n for n, use in enumerate(aux_uses())}


def mixer_outputs():
    made, panel, half_open = {}, MIX_P, {}
    for step in MIXER:
        if step[0] not in ("qkv", "z", "fourier_in", "gate", "branch", "sconv"):
            continue
        if step[0] == "branch" and step[2] % 2:
            made[step] = MIX_O + len(made), half_open[step[1]], 1
            continue
        made[step] = MIX_O + len(made), panel, 0
        if step[0] == "branch":
            half_open[step[1]] = panel
        panel += 1
    return made


MIX_OUT = mixer_outputs()
HALVES = 12


W_OUT = [(i, 0) for i in range(4)] + [(i, 1) for i in range(4)] + [(i, half) for i in range(4, 8) for half in range(2)]


def passes():
    out, panel, n = {}, {}, 0
    for i in range(56):
        n += 1
        out[MEM_O + i] = panel[MEM_P + i] = n
    for k, (i, _) in enumerate(W_OUT):
        n += 1
        out[WOUT_O + i] = panel[WOUT_P + k] = n
    for first_o, first_p, count, each in ((UP1_O, UP1_P, UP, 1), (DOWN1_O, DOWN1_P, 8, 3)):
        for i in range(count):
            for j in range(each):
                n += 1
                panel[first_p + i * each + j] = n
            out[first_o + i] = n
    for o, p, _ in MIX_OUT.values():
        n += 1
        out[o] = panel[p] = n
    for first_o, first_p, count, each in ((OUT2_O, OUT2_P, 8, 1), (UP2_O, UP2_P, UP, 1), (DOWN2_O, DOWN2_P, 8, 3)):
        for i in range(count):
            for j in range(each):
                n += 1
                panel[first_p + i * each + j] = n
            out[first_o + i] = n
    return out, panel


OUT_PASS, PANEL_PASS = passes()


class Order:

    def __init__(self, engine, semaphore):
        self.engine, self.semaphore, self.count = engine, semaphore, 0

    def __call__(self, instruction):
        self.count += 1
        instruction.then_inc(self.semaphore, 1)
        self.engine.wait_ge(self.semaphore, self.count)


def build(nc, a):
    f32, f32r, i32 = mybir.dt.float32, mybir.dt.float32r, mybir.dt.int32
    ALU, ACT, AX = mybir.AluOpType, mybir.ActivationFunctionType, mybir.AxisListType
    ctx = ExitStack()
    with ctx:
        base = 16512
        WORDS = (229368 - base) // 4
        ctx.enter_context(nc.sbuf_tensor("fence", [P, WORDS - 8], f32))

        def at(name, word, shape, dtype=f32):
            words = 1
            for n in shape[1:]:
                words *= n
            assert word + words <= WORDS - 8, (name, word, words)
            return nc.alloc_sbuf_tensor_at(name, shape, dtype, offset=base + 4 * word)

        top = 0

        def take(words):
            nonlocal top
            top += (words + 7) // 8 * 8
            return top - (words + 7) // 8 * 8

        raw = at("raw", take(RING * 1024), [P, RING, 1024])
        whi = at("whi", take(RING * 1024), [P, RING, 1024], f32r)
        wlo = at("wlo", take(RING * 1024), [P, RING, 1024], f32r)
        xh = at("xh", take(KT * LEN), [P, KT, LEN], f32r)
        xl = at("xl", take(KT * LEN), [P, KT, LEN], f32r)
        h_at, tmp_at, sq_at = take(KT * LEN), take(KT * LEN), take(KT * LEN)
        h = at("h", h_at, [P, KT, LEN])
        tmp = at("tmp", tmp_at, [P, KT, LEN])
        sq = at("sq", sq_at, [P, KT, LEN])
        lnt_at, rstd_at = take(512), take(512)
        lnt = at("lnt", lnt_at, [P, 512])
        rstd = at("rstd", rstd_at, [P, 512])
        xrstd = at("xrstd", take(LEN), [P, LEN])
        ident = at("ident", take(P), [P, P])
        ones = at("ones", take(P), [P, P])
        vec = at("vec", take(VECS + 1), [P, VECS + 1])
        fmat = at("fmat", take(2 * P), [P, 2 * P])
        wba = at("wba", take(P), [P, KT, 16])
        tri = at("tri", take(2 * CH), [CH, 2, CH])
        lvl = at("lvl", take(2 * CH), [CH, 2, CH])
        eye17 = at("eye17", take(SUB * SUB), [P, SUB, SUB])
        late = take(2048)
        masks = at("masks", late, [P, 8, P], i32)
        upw = at("upw", late + 1024, [16, 512])
        wglr = at("wglr", late + 1536, [P, KT, 16])
        cmat = at("cmat", late, [CH, NC, 2, ROWS])
        ar = top
        hh = at("hh", ar, [P, FT, LEN], f32r)
        hl = at("hl", ar + FT * LEN, [P, FT, LEN], f32r)
        sil = at("sil", ar + 2 * FT * LEN, [P, 2, LEN])
        hid = at("hid", ar + 2 * FT * LEN + 2 * LEN, [P, 2, LEN])
        q = at("q", ar, [P, HEADS, ROWS])
        k = at("k", ar + 2048, [P, HEADS, ROWS])
        f = at("f", ar + 4096, [P, HEADS, ROWS])
        tot = at("tot", ar + 6144, [P, HEADS, ROWS])
        memh = at("memh", ar, [P, KT, ROWS], f32r)
        meml = at("meml", ar + 2048, [P, KT, ROWS], f32r)
        mixh = at("mixh", ar, [P, 16, ROWS], f32r)
        mixl = at("mixl", ar + 4096, [P, 16, ROWS], f32r)
        v = at("v", ar + 8192, [P, 2, 1536])
        s = at("s", ar + 11264, [P, HEADS, ROWS])
        memx = at("memx", ar + 11264, [P, KT, ROWS])
        s3 = at("s3", ar + 13312, [P, HEADS, P])
        mk = at("mk", ar + 14336, [P, 4, ROWS])
        mv = at("mv", ar + 15360, [P, 2, 512])
        xq = at("xq", ar + 16384, [P, 4, ROWS])
        gate = at("gate", ar + 17408, [P, 16, ROWS])
        ot = at("ot", ar + 21504, [P, 4, 2, ROWS])
        prob = at("prob", ar + 23552, [P, 2, 2, ROWS])
        glr = at("glr", ar + 24576, [16, ROWS])
        small1 = at("small1", ar + 24832, [P, 64])
        pt = at("pt", tmp_at, [P, 4, 2, ROWS])
        sqo = at("sqo", sq_at, [P, 4, 2, ROWS])
        qkv = at("qkv", ar, [P, 12, LEN])
        qn, kn, vf = qkv[:, 0:4, :], qkv[:, 4:8, :], qkv[:, 8:12, :]
        pre = at("pre", ar + 3264, [P, 12, LEN])
        dmat = at("dmat", ar + 3264, [CH, 2, 2, 4, CH])
        aoff = at("aoff", ar + 4352, [CH, 2, 4, CH])
        xm = at("xm", ar + 4896, [CH, 2, 4, CH])
        state = at("state", ar + 3264, [P, 2, 4, P])
        rr = at("rr", ar + 4288, [CH, 2, 4, P])
        vnew = at("vnew", ar + 5312, [CH, 2, 4, P])
        vdec = at("vdec", ar + 2176, [CH, 2, 4, P])
        vt = at("vt", ar + 6528, [CH, NC, 4, P])
        kt = at("kt", ar + 8576, [CH, NC, 4, P])
        eg = at("eg", ar + 10624, [P, 8, 4, CH])
        att = at("att", ar + 12800, [CH, 8, 4, CH])
        am = at("am", ar + 14976, [CH, 8, 4, CH])
        od = at("od", ar + 14976, [P, 4, LEN])
        tm = at("tm", ar + 17152, [CH, 8, 4, CH])
        um = at("um", ar + 19328, [CH, 8, 4, CH])
        mg = at("mg", ar + 21504, [P, KT, ROWS])
        zs = at("zs", ar + 23552, [P, 4, ROWS])
        small2 = at("small2", ar + 24576, [P, 424])
        gt = at("gt", rstd_at, [P, 2, ROWS])
        ba = at("ba", lnt_at, [16, LEN])
        yh = at("yh", tmp_at, [P, 4, ROWS], f32r)
        yl = at("yl", tmp_at + 1024, [P, 4, ROWS], f32r)
        pf = at("pf", h_at, [CH, 2, NC, 2 * P])
        sc = at("sc", h_at, [P, 2, 3, LEN])
        drs = at("drs", h_at + 6 * LEN, [P, 2 * ROWS])
        fu = at("fu", ar + 21504, [P, 4, LEN])
        cc = at("cc", sq_at, [P, 2, 2, LEN])
        bn = at("bn", sq_at + 1088, [P, SUB, SUB])
        tb = at("tb", sq_at + 1384, [P, SUB, SUB])
        pr = at("pr", sq_at + 1680, [P, SUB * SUB])
        dsq = at("dsq", ar + 0, [P, 4, ROWS])
        yd = at("yd", ar + 1088, [P, 4, ROWS])

        logit_a = small2[0:CH, 0:32].rearrange("p (c e) -> p c e", c=NC)
        abs_a = small2[0:CH, 32:64].rearrange("p (c e) -> p c e", c=NC)
        beta = small2[0:CH, 64:96].rearrange("p (c e) -> p c e", c=NC)
        grate = small2[0:CH, 96:128].rearrange("p (c e) -> p c e", c=NC)
        ea = small2[0:CH, 128:136]
        gc = small2[0:CH, 136:168].rearrange("p (d c h) -> p d c h", d=2, c=NC)
        gtot = small2[0:CH, 168:200].rearrange("p (c d h) -> p c d h", d=2, c=NC)
        nec = small2[0:CH, 200:232].rearrange("p (d c h) -> p d c h", d=2, c=NC)
        ed = small2[0:CH, 232:264].rearrange("p (d c h) -> p d c h", d=2, c=NC)
        elast = small2[:, 264:296].rearrange("p (u h) -> p u h", u=8)
        lb_m, lb_e, lb_s = small1[:, 0:4], small1[:, 4:8], small1[:, 8:12]
        lb_fl, lb_1m = small1[:, 12:16], small1[:, 16:20]
        mx, nmx, rs, ri = (small1[:, 20 + 8 * n:28 + 8 * n] for n in range(4))

        pb = [ctx.enter_context(nc.psum_tensor(f"panel{i}", [P, 512], f32)) for i in range(4)]
        ab = [ctx.enter_context(nc.psum_tensor(f"aux{i}", [P, 512], f32)) for i in range(4)]

        def vcol(name, n=0, parts=P):
            c = VEC_AT[name] + n
            return vec[0:parts, c:c + 1]

        def sem(name):
            return ctx.enter_context(nc.semaphore(name))

        hi_ready = sem("hi_ready")
        lo_ready = sem("lo_ready")
        passed = sem("passed")
        aux_full = sem("aux_full")
        vec_in = sem("vec_in")
        ones_in = sem("ones_in")
        more_in = sem("more_in")
        mem_in = sem("mem_in")
        x_in = sem("x_in")
        late_in = sem("late_in")
        stored = sem("stored")
        h_saved = sem("h_saved")
        h_back = sem("h_back")
        eps_set = sem("eps_set")
        squared = sem("squared")
        summed = sem("summed")
        last_squared = sem("last_squared")
        scaled = sem("scaled")
        wba_scaled = sem("wba_scaled")
        gate_ready = sem("gate_ready")
        z_ready = sem("z_ready")
        sil_ready = sem("sil_ready")
        hid_ready = sem("hid_ready")
        split_high = sem("split_high")
        split_low = sem("split_low")
        rstd_ready = sem("rstd_ready")
        h_ready = sem("h_ready")
        weighed = sem("weighed")
        dve_order = sem("dve_order")
        act_order = sem("act_order")
        pool_order = sem("pool_order")
        s_zero = sem("s_zero")
        lb_shifted = sem("lb_shifted")
        lb_exp = sem("lb_exp")
        u_ready = sem("u_ready")
        u_exp = sem("u_exp")
        a_ready = sem("a_ready")
        qk_ready = sem("qk_ready")
        max_ready = sem("max_ready")
        prob_ready = sem("prob_ready")
        o_squared = sem("o_squared")
        o_mixed = sem("o_mixed")
        o_rstd = sem("o_rstd")
        mix_high = sem("mix_high")
        mix_low = sem("mix_low")
        hid_high = sem("hid_high")
        hid_low = sem("hid_low")
        a_logit = sem("a_logit")
        a_soft = sem("a_soft")
        g_ready = sem("g_ready")
        ec_ready = sem("ec_ready")
        ed_ready = sem("ed_ready")
        td_ready = sem("td_ready")
        tap1 = sem("tap1")
        tap2 = sem("tap2")
        conv_done = sem("conv_done")
        silu_qkv = sem("silu_qkv")
        qk_squared = sem("qk_squared")
        l2_rstd = sem("l2_rstd")
        qk_normed = sem("qk_normed")
        row_exp = sem("row_exp")
        diff_ready = sem("diff_ready")
        decay_ready = sem("decay_ready")
        am_raw = sem("am_raw")
        am_ready = sem("am_ready")
        att_raw = sem("att_raw")
        att_ready = sem("att_ready")
        qe_ready = sem("qe_ready")
        tm_zero = sem("tm_zero")
        blocks_in = sem("blocks_in")
        blocks_out = sem("blocks_out")
        inverse_ready = sem("inverse_ready")
        aoff_ready = sem("aoff_ready")
        um_ready = sem("um_ready")
        vdec_ready = sem("vdec_ready")
        y_high = sem("y_high")
        y_low = sem("y_low")
        yc_ready = sem("yc_ready")
        yd_ready = sem("yd_ready")
        dsq_ready = sem("dsq_ready")
        drs_ready = sem("drs_ready")
        mg_ready = sem("mg_ready")
        mg_high = sem("mg_high")
        mg_low = sem("mg_low")
        raw_ready = [sem(f"raw_ready{i}") for i in range(RING)]
        bank_free = [sem(f"bank_free{i}") for i in range(4)]
        aux_free = [sem(f"aux_free{i}") for i in range(4)]
        level_up = [sem(f"level_up{i}") for i in range(2)]
        SCALE = float(P) ** -0.5
        TOT = {2: 0, 3: 128, 4: 192, 5: 224, 6: 240, 7: 248}

        def aux(*use):
            n = AUX[use]
            return ab[n % 4], n

        def aux_open(n):
            if n >= 4:
                nc.tensor.wait_ge(aux_free[n % 4], n // 4)

        def aux_wait(eng, n):
            eng.wait_ge(aux_full, n + 1)

        def aux_freed(eng, n):
            eng.wait_ge(aux_free[n % 4], n // 4 + 1)

        def bank_freed(eng, o):
            eng.wait_ge(bank_free[o % 4], o // 4 + 1)

        def bc(ap, axis, n):
            ap = ap.unsqueeze(axis)
            shape = list(ap.shape)
            shape[axis] = n
            return ap.to_broadcast(shape)

        W = [ROWS, ROWS, ROWS, LEN, LEN, LEN, ROWS, ROWS, ROWS]
        SPLIT = {0: 0, 1: 1, 3: 2, 5: 3, 7: 4}

        def hcol(w):
            return slice(LEN - w, LEN)

        def squares_of(n):
            return tmp if n == 1 else sq

        def norm_source(n):
            if n == 0:
                return memx[:]
            return tmp[:, :, 0:W[n]] if n in (4, 6, 8) else h[:, :, hcol(W[n])]

        block = ctx.enter_context(nc.Block())

        @block.sync
        def _(sp):
            sp.dma_start(vec[:, 0:VECS], a["vec"]).then_inc(vec_in, 16)
            sp.dma_start(memx[:], a["mem"]).then_inc(mem_in, 16)
            sp.dma_start(raw[:, 0, :], a["panels"][0]).then_inc(raw_ready[0], 16)
            sp.dma_start(ones[:], a["ones"]).then_inc(ones_in, 16)
            sp.dma_start(h[:, :, META:LEN], a["x"]).then_inc(x_in, 16)
            for r in range(1, RING):
                sp.dma_start(raw[:, r, :], a["panels"][r]).then_inc(raw_ready[r], 16)
            for name, dst in (("wglr", wglr[:]), ("upw", upw[:]), ("wba", wba[:]), ("masks", masks[:]), ("ident", ident[:]),
                              ("tri", tri[:]), ("lvl", lvl[:]), ("eye17", eye17[:]), ("fmat", fmat[:]), ("meta", h[:, :, 0:META])):
                sp.dma_start(dst, a[name]).then_inc(more_in, 16)

            def panels(first, last, row0):
                with sp.Fori(0, (last - first) // RING) as g:
                    for r in range(RING):
                        row = sp.snap(g * RING + (row0 + r))
                        sp.wait_ge(lo_ready, g * RING + (first + r - RING + 1))
                        sp.dma_start(raw[:, r, :], a["panels"][row]).then_inc(raw_ready[r], 16)

            def down(layer, first):
                with sp.Fori(0, 2) as g:
                    for n in range(12):
                        r, part = n % RING, n % 3
                        lo, size = (0, 1024, 1920)[part], (1024, 896, 896)[part]
                        row = sp.snap(g * 4 + (layer * 8 + n // 3))
                        sp.wait_ge(lo_ready, g * 12 + (first + n - RING + 1))
                        sp.dma_start(raw[:, r, 0:size], a["down"][row][:, lo:lo + size]).then_inc(raw_ready[r], 16)

            panels(RING, DOWN1_P, RING)
            down(0, DOWN1_P)
            panels(MIX_P, DOWN2_P, MIX_P - 24)
            down(1, DOWN2_P)
            for half in range(2):
                sp.wait_ge(h_ready, 8 * 3 + 4 * half + 4)
                sp.dma_start(a["out"][:, 4 * half:4 * half + 4, :], h[:, 4 * half:4 * half + 4, META:LEN]).then_inc(stored, 16)
            sp.wait_ge(stored, 32)

        @block.gpsimd
        def _(pool):
            order = Order(pool, pool_order)
            split = [0]

            def low(panel, slot):
                pool.wait_ge(hi_ready, panel)
                nc.gpsimd.tensor_tensor(wlo[:, slot, :], raw[:, slot, :], whi[:, slot, :].bitcast(f32),
                                        ALU.subtract).then_inc(lo_ready, 1)

            def ahead(panel):
                while split[0] <= min(panel + LEAD, PANELS - 1):
                    low(split[0] + 1, split[0] % RING)
                    split[0] += 1

            def loop(count):
                first = split[0]
                with pool.Fori(0, count // RING) as g:
                    for n in range(RING):
                        low(g * RING + (first + n + 1), (first + n) % RING)
                split[0] += count

            def sum_squares(n):
                for kk in range(1, KT):
                    pool.wait_ge(squared, 8 * SPLIT[n] + kk + 1)
                    ins = nc.gpsimd.tensor_tensor(sq[:, 0, 0:W[n]], sq[:, 0, 0:W[n]], sq[:, kk, 0:W[n]], ALU.add)
                    if kk < KT - 1:
                        order(ins)
                ins.then_inc(summed, 1)

            for o in range(8):
                ahead(MEM_P + o)
            pool.wait_ge(split_low, 8)
            nc.gpsimd.memset(s[:], 0.0).then_inc(s_zero, 1)
            for step in FIRST:
                if step[0] == "out":
                    ahead(IN_P + step[1])
                if step[0] == "wout":
                    ahead(WOUT_P + step[1])
            ahead(WOUT_P + 15)
            sum_squares(3)
            loop(UP + 24)
            sum_squares(5)
            for step in MIXER:
                kind, u = step[0], step[-1]
                if step in MIX_OUT:
                    ahead(MIX_OUT[step][1])
                if step == ("cumulate",):
                    pool.wait_ge(g_ready, 1)
                    nc.gpsimd.memset(tm[:], 0.0).then_inc(tm_zero, 1)
                if kind == "chunk":
                    for d in range(2):
                        unit = 2 * u + d
                        if d:
                            aux_freed(pool, AUX[("kk", u)])
                        else:
                            pool.wait_ge(am_raw, u + 1)
                        nc.gpsimd.tensor_tensor(am[:, unit], am[:, unit], bc(beta[:, u, 4 * d:4 * d + 4], 2, CH),
                                                ALU.mult).then_inc(am_ready, 1)
                        if d:
                            aux_freed(pool, AUX[("qk", u)])
                        else:
                            pool.wait_ge(att_raw, u + 1)
                        nc.gpsimd.tensor_tensor(att[:, unit], att[:, unit], bc(tri[:, d, :], 1, 4),
                                                ALU.mult).then_inc(att_ready, 1)
                        pool.wait_ge(row_exp, unit + 1)
                        order(nc.gpsimd.tensor_copy(elast[:, unit, :], eg[:, unit, :, 0 if d else CH - 1]))
                        nc.gpsimd.tensor_tensor(eg[:, unit], eg[:, unit], qn[:, :, CH * u:CH * u + CH],
                                                ALU.mult).then_inc(qe_ready, 1)
                if kind == "vn" and u < NC - 1:
                    for d in range(2):
                        c = NC - 1 - u if d else u
                        aux_freed(pool, AUX[("vn", u, d)])
                        if u:
                            aux_wait(pool, AUX[("su", u - 1, d)])
                        nc.gpsimd.tensor_tensor(vdec[:, d], vnew[:, d], bc(ed[:, d, c, :], 2, P),
                                                ALU.mult).then_inc(vdec_ready, 1)
            ahead(OUT2_P + 7)
            sum_squares(7)
            loop(PANELS - split[0] - (PANELS - split[0]) % RING)
            ahead(PANELS - 1)

        @block.scalar
        def _(act):
            order = Order(act, act_order)
            nxt = [0]
            LN_EXP, SILU = "natural_log_exp_and_others", "silu_and_others"
            A = nc.scalar.activation

            def high(raw_count, used, slot):
                act.wait_ge(raw_ready[slot], raw_count)
                if used is not None:
                    act.wait_ge(passed, used)
                A(whi[:, slot, :], raw[:, slot, :], ACT.Copy).then_inc(hi_ready, 1)

            def ahead(panel):
                while nxt[0] <= min(panel + LEAD, PANELS - 1):
                    p = nxt[0]
                    high(16 * (p // RING + 1), PANEL_PASS[p - RING] if p >= RING else None, p % RING)
                    nxt[0] += 1

            def high_in_loop(g, per_turn, n):
                p = nxt[0] + n
                high(g * (16 * per_turn // RING) + 16 * (p // RING + 1), g * per_turn + PANEL_PASS[p - RING], p % RING)

            def out_wait(o):
                act.wait_ge(passed, OUT_PASS[o])

            eps = vec[:, VECS:VECS + 1]

            def root(bank, n, w, count, dst):
                aux_wait(act, n)
                A(lnt[:, 0:w], bank[:, 0:w], ACT.Ln, scale=1.0 / count, bias=eps).then_inc(aux_free[n % 4], 1)
                aux_freed(act, n)
                return A(dst[:, 0:w], lnt[:, 0:w], ACT.Exp, scale=-0.5)

            def squares(n):
                for kk in range(KT):
                    A(squares_of(n)[:, kk, 0:W[n]], norm_source(n)[:, kk, :], ACT.Square).then_inc(squared, 1)

            def post_root(n):
                bank, use = aux("stat", n)
                root(bank, use, W[n], 1024.0, rstd).then_inc(rstd_ready, 1)

            def pre_norm(n, ready, name, at0, last_out=None):
                w, src = W[n], norm_source(n)
                if last_out is not None:
                    out_wait(last_out)
                for kk in range(KT):
                    ready(kk)
                    A(xh[:, kk, 0:w], src[:, kk, :], ACT.Identity, scale=vcol(name, at0 + kk)).then_inc(split_high, 1)
                    A(sq[:, kk, 0:w], src[:, kk, :], ACT.Square).then_inc(squared, 1)

            def pre_root(n):
                bank, use = aux("stat", n)
                root(bank, use, W[n] + (2 if n == 0 else 0), 1024.0, xrstd).then_inc(rstd_ready, 1)

            def combined(n):
                return lambda kk: act.wait_ge(h_ready, 8 * n + kk + 1)

            nc.scalar.preload_act_table_set(LN_EXP)
            act.wait_ge(vec_in, 16)
            act.wait_ge(mem_in, 16)
            for kk in range(KT):
                A(memh[:, kk, :], memx[:, kk, :], ACT.Identity, scale=vcol("mem_norm", kk)).then_inc(split_high, 1)
            high(16, None, 0)
            nxt[0] = 1
            squares(0)
            ahead(MEM_P + 1 - LEAD)
            act.wait_ge(x_in, 16)
            squares(1)
            act.wait_ge(eps_set, 1)
            pre_root(0)
            ahead(MEM_P)
            act.wait_ge(rstd_ready, 1)
            post_root(1)
            for kk in range(KT):
                act.wait_ge(scaled, kk + 1)
                A(xh[:, kk, 0:ROWS], tmp[:, kk, 0:ROWS], ACT.Copy).then_inc(split_high, 1)
                if kk == 3:
                    ahead(MEM_P + 1)
            for o in range(2, 8):
                ahead(MEM_P + o)
            act.wait_ge(lb_shifted, 1)
            A(lb_e, lb_m, ACT.Exp).then_inc(lb_exp, 1)

            for step in FIRST:
                kind, i = step[0], step[-1]
                if kind == "out":
                    ahead(IN_P + i)
                    o = IN_O + i
                    if i < 4:
                        out_wait(o)
                        order(A(f[:, 4 + i, :], pb[o % 4][:, 0:ROWS], ACT.Sigmoid))
                        A(k[:, 4 + i, :], pb[o % 4][:, 0:ROWS], ACT.Sigmoid, scale=-1.0).then_inc(bank_free[o % 4], 1)
                    if GATE <= i < V:
                        out_wait(o)
                        A(gate[:, i - GATE, :], pb[o % 4][:, 0:ROWS], ACT.Silu).then_inc(bank_free[o % 4], 1)
                if kind == "decay":
                    nc.scalar.preload_act_table_set(LN_EXP)
                    act.wait_ge(u_ready, 1)
                    order(A(tot[:, 0:4, :], tot[:, 0:4, :], ACT.Exp, scale=-1.0))
                    A(tot[:, 0:4, :], tot[:, 0:4, :], ACT.Ln, bias=1.0).then_inc(u_exp, 1)
                    act.wait_ge(u_ready, 2)
                    A(f[:, 0:4, :], f[:, 0:4, :], ACT.Exp, scale=1.0 / 16.0).then_inc(a_ready, 1)
                if kind == "wout":
                    ahead(WOUT_P + i)
                if kind == "scores":
                    if i == 0:
                        nc.scalar.preload_act_table_set(LN_EXP)
                    bank, n = aux("scores", i)
                    act.wait_ge(max_ready, i + 1)
                    for e in range(2):
                        ins = A(prob[:, i % 2, e, :], bank[:, 256 * e:256 * e + 256], ACT.Exp, scale=SCALE,
                                bias=nmx[:, 2 * i + e:2 * i + e + 1], accum_out=rs[:, 2 * i + e:2 * i + e + 1])
                    ins.then_inc(aux_free[n % 4], 1)
                if kind == "o":
                    aux_freed(act, AUX[step])
                    if i >= 4:
                        aux_wait(act, AUX[("o_norm", i - 4)])
                    A(sqo[:, i % 4], ot[:, i % 4], ACT.Square).then_inc(o_squared, 1)
                if kind == "o_norm":
                    bank, n = aux("o_norm", i)
                    w, count = (ROWS, 256.0) if i < 4 else (2 * ROWS, 128.0)
                    aux_wait(act, n)
                    if i:
                        act.wait_ge(o_mixed, i)
                    root(bank, n, w, count, rstd).then_inc(o_rstd, 1)
                if kind == "o_split":
                    act.wait_ge(o_mixed, i + 1)
                    A(mixh[:, 2 * i:2 * i + 2, :], ot[:, i % 4], ACT.Copy).then_inc(mix_high, 1)
            for m in range(4, 16):
                ahead(WOUT_P + m)

            post_root(2)
            act.dma_start(cmat[:], a["cmat"]).then_inc(late_in, 16)
            act.wait_ge(more_in, 10 * 16)
            pre_norm(3, combined(0), "gains", 0, WOUT_O + 7)
            pre_root(3)

            def up_loop(layer, first_o, w):
                nc.scalar.preload_act_table_set(SILU)
                with act.Fori(0, UP // 4) as g:
                    for pair in range(2):
                        high_in_loop(g, 4, 2 * pair)
                        high_in_loop(g, 4, 2 * pair + 1)
                        tile = act.snap(g * 2 + pair)
                        act.wait_ge(bank_free[2 * pair], g + (first_o // 4 + 1))
                        A(sil[:, pair, 0:w], sil[:, pair, 0:w], ACT.Silu).then_inc(sil_ready, 1)
                        act.wait_ge(hid_ready, g * 2 + (layer * FT + pair + 1))
                        A(hh[:, bass.ds(tile, 1), 0:w].rearrange("p a s -> p (a s)"), hid[:, pair, 0:w],
                          ACT.Copy).then_inc(hid_high, 1)
                nxt[0] += UP

            ahead(UP1_P - 1)
            up_loop(0, UP1_O, LEN)
            with act.Fori(0, 2) as g:
                for n in range(12):
                    high_in_loop(g, 12, n)
            nxt[0] += 24
            nc.scalar.preload_act_table_set(LN_EXP)
            post_root(4)
            pre_norm(5, combined(1), "gains", 16, DOWN1_O + 7)
            pre_root(5)
            act.dma_start(a["spill"], h[:, :, META:LEN]).then_inc(h_saved, 16)

            for step in MIXER:
                kind, i = step[0], step[-1]
                if step in MIX_OUT:
                    o, p, half = MIX_OUT[step]
                    ahead(p)
                    bank = pb[o % 4]
                if kind == "logits":
                    bank, n = aux("logits")
                    act.wait_ge(a_logit, 1)
                    A(beta, bank[0:CH, 0:64].rearrange("p (c e) -> p c e", c=NC)[:, :, 0:8], ACT.Sigmoid)\
                        .then_inc(aux_free[n % 4], 1)
                    nc.scalar.preload_act_table_set(LN_EXP)
                    A(ea, vec[0:CH, VEC_AT["a_log"]:VEC_AT["a_log"] + 8], ACT.Exp)
                    act.wait_ge(a_logit, 2)
                    order(A(abs_a, abs_a, ACT.Exp, scale=-1.0))
                    A(abs_a, abs_a, ACT.Ln, bias=1.0).then_inc(a_soft, 1)
                if kind == "cumulate":
                    aux_freed(act, AUX[("cumulate",)])
                    A(small2[0:CH, 200:232], small2[0:CH, 136:168], ACT.Exp).then_inc(ec_ready, 1)
                    act.wait_ge(td_ready, 1)
                    A(small2[0:CH, 232:264], small2[0:CH, 232:264], ACT.Exp).then_inc(ed_ready, 1)
                if kind == "silu":
                    if i == 0:
                        nc.scalar.preload_act_table_set(SILU)
                    act.wait_ge(conv_done, 4 * i + 4)
                    part = slice(4 * i, 4 * i + 4)
                    A(qkv[:, part, :], qkv[:, part, :], ACT.Silu).then_inc(silu_qkv, 1)
                    if i < 2:
                        act.wait_ge(silu_qkv, i + 1)
                        A(sq[:, part, :], qkv[:, part, :], ACT.Square).then_inc(qk_squared, 1)
                if kind == "l2norm":
                    nc.scalar.preload_act_table_set(LN_EXP)
                    for t in range(8):
                        bank, n = aux("l2", t)
                        aux_wait(act, n)
                        A(sq[:, t, :], bank[:, 0:LEN], ACT.Ln, bias=eps).then_inc(aux_free[n % 4], 1)
                    for t in (4, 5, 6, 7):
                        aux_freed(act, AUX[("l2", t)])
                    A(sq[:], sq[:], ACT.Exp, scale=-0.5).then_inc(l2_rstd, 1)
                if kind == "chunk":
                    for use, dst in (("kt", kt), ("vt", vt)):
                        bank, n = aux(use, i)
                        aux_wait(act, n)
                        A(dst[:, i].rearrange("p h d -> p (h d)"), bank[0:CH, :], ACT.Copy).then_inc(aux_free[n % 4], 1)
                    for d in range(2):
                        bank, n = aux(f"row{d}", i)
                        aux_wait(act, n)
                        A(eg[:, 2 * i + d].rearrange("p h t -> p (h t)"), bank[:, 0:4 * CH], ACT.Exp).then_inc(row_exp, 1)
                    for d in range(2):
                        act.wait_ge(diff_ready, 2 * i + d + 1)
                        if d == 0:
                            A(dmat[:, d, 1], dmat[:, d, 1], ACT.Exp)
                        A(dmat[:, d, 0], dmat[:, d, 0], ACT.Exp, scale=-1.0).then_inc(decay_ready, 1)
                if kind == "gather":
                    act.wait_ge(am_ready, 8)
                    act.wait_ge(qk_normed, 2)
                    for b in range(4):
                        at_b = slice(SUB * b, SUB * b + SUB)
                        act.dma_start(a["blocks"][b].rearrange("m i j -> i m j"),
                                      am[at_b, :, :, at_b].rearrange("i u h j -> i (u h) j")).then_inc(blocks_in, 16)
                if kind == "blocks":
                    act.wait_ge(blocks_in, 64)
                    act.dma_start(bn[:], a["blocks"].rearrange("b m i j -> (b m) i j")).then_inc(blocks_in, 16)
                if kind == "inverses":
                    act.wait_ge(inverse_ready, 1)
                    act.dma_start(a["inverses"].rearrange("b m i j -> (b m) i j"), tb[:]).then_inc(blocks_out, 16)
                if kind == "scatter":
                    act.wait_ge(tm_zero, 1)
                    act.wait_ge(blocks_out, 16)
                    for b in range(4):
                        at_b = slice(SUB * b, SUB * b + SUB)
                        act.dma_start(tm[at_b, :, :, at_b].rearrange("i u h j -> i (u h) j"),
                                      a["inverses"][b].rearrange("m i j -> i m j")).then_inc(blocks_out, 16)
                if step == ("dft", 0):
                    bank_freed(act, MIX_OUT[("z", 3)][0])
                    A(zs[:], zs[:], ACT.Silu).then_inc(z_ready, 1)
                if kind == "dft":
                    bank, n = aux("dft_out", i)
                    aux_wait(act, n)
                    A(yh[:, i, :], bank[:, 0:ROWS], ACT.Copy).then_inc(y_high, 1)
                if kind == "gate":
                    g = 8 * step[1] + i
                    bank_freed(act, o)
                    A(gt[:, g % 2, :], gt[:, g % 2, :], ACT.Sigmoid).then_inc(gate_ready, 1)
                if kind == "sconv" and i == 2:
                    act.wait_ge(yc_ready, step[1] + 1)
                    out_wait(MIX_OUT[("branch", 0, 7)][0])
                    A(yh[:, step[1], :], cc[:, step[1] % 2, 1, 0:ROWS], ACT.Copy).then_inc(y_high, 1)
                if kind in ("u0", "u17"):
                    bank, n = aux(kind, i)
                    aux_wait(act, n)
                    A(um[:, i].rearrange("p h t -> p (h t)"), bank[0:CH, 0:4 * CH], ACT.Copy).then_inc(aux_free[n % 4], 1)
                if kind in ("x17", "x34"):
                    bank, n = aux(kind, i)
                    aux_wait(act, n)
                    A(xm[:, i % 2].rearrange("p h t -> p (h t)"), bank[0:CH, 0:4 * CH], ACT.Copy).then_inc(aux_free[n % 4], 1)
                if kind == "vn":
                    bank, n = aux("vn", i, 0)
                    aux_wait(act, n)
                    if 0 < i < NC - 1:
                        act.wait_ge(vdec_ready, 2 * i)
                    A(vnew[:, 0].rearrange("p h d -> p (h d)"), bank[0:CH, :], ACT.Copy).then_inc(aux_free[n % 4], 1)
                if kind == "delta_norm":
                    nc.scalar.preload_act_table_set(LN_EXP)
                    aux_freed(act, AUX[("od", NC - 1, 0)])
                    aux_freed(act, AUX[("od", NC - 1, 1)])
                    A(dsq[:], od[:, :, META:LEN], ACT.Square).then_inc(dsq_ready, 1)
                    for e in range(2):
                        bank, n = aux("dstat", e)
                        aux_wait(act, n)
                        if e:
                            act.wait_ge(yd_ready, 1)
                        root(bank, n, 2 * ROWS, 128.0, drs).then_inc(drs_ready, 1)
                    for e in range(4):
                        if e % 2 == 0:
                            act.wait_ge(yd_ready, e // 2 + 1)
                        if e == 0:
                            out_wait(MIX_OUT[("branch", 1, 7)][0])
                        A(yh[:, e, :], yd[:, e, :], ACT.Copy).then_inc(y_high, 1)
            act.wait_ge(yc_ready, 4)
            act.dma_start(h[:, :, META:LEN], a["spill"]).then_inc(h_back, 16)
            out_wait(MIX_OUT[("gate", 2, 7)][0])
            for kk in range(KT):
                act.wait_ge(mg_ready, 8 + kk + 1)
                if kk == 0:
                    out_wait(MIX_OUT[("branch", 2, 7)][0])
                A(xh[:, kk, 0:ROWS], mg[:, kk, :], ACT.Copy).then_inc(mg_high, 1)
            for o in range(8):
                ahead(OUT2_P + o)
            nc.scalar.preload_act_table_set(LN_EXP)
            post_root(6)
            pre_norm(7, combined(2), "gains", 32, OUT2_O + 7)
            pre_root(7)
            ahead(UP2_P - 1)
            up_loop(1, UP2_O, ROWS)
            ahead(PANELS - 1)
            nc.scalar.preload_act_table_set(LN_EXP)
            post_root(8)

        @block.vector
        def _(dve):
            order = Order(dve, dve_order)
            TT, TS, STT, CP = (nc.vector.tensor_tensor, nc.vector.tensor_scalar,
                               nc.vector.scalar_tensor_tensor, nc.vector.tensor_copy)

            def out_wait(o):
                dve.wait_ge(passed, OUT_PASS[o])

            def low_part(n, kk, name, at0):
                src, hi_, lo_ = (memx, memh, meml) if n == 0 else (h[:, :, hcol(W[n])], xh, xl)
                dve.wait_ge(split_high, 8 * SPLIT[n] + kk + 1)
                STT(lo_[:, kk, 0:W[n]], src[:, kk, :], vcol(name, at0 + kk), hi_[:, kk, 0:W[n]].bitcast(f32),
                    ALU.mult, ALU.subtract).then_inc(split_low, 1)

            def combine(n, at0, factor, following=None):
                w = W[n]
                dve.wait_ge(rstd_ready, n + 1)
                for t in range(KT + 2):
                    if t < KT:
                        STT(tmp[:, t, 0:w], tmp[:, t, 0:w], vcol("gains", at0 + t), rstd[:, 0:w], ALU.mult, ALU.mult)\
                            .then_inc(weighed, 1)
                    kk = t - 1
                    if 0 <= kk < KT:
                        dve.wait_ge(weighed, 8 * (n // 2 - 2) + kk + 1)
                        STT(h[:, kk, hcol(w)], tmp[:, kk, 0:w], factor, h[:, kk, hcol(w)], ALU.mult, ALU.add).then_inc(h_ready, 1)
                    kk = t - 2
                    if following is not None and kk >= 0:
                        low_part(following, kk, "gains", at0 + 8)

            nc.vector.memset(vec[:, VECS:VECS + 1], EPS).then_inc(eps_set, 1)

            def add_squares(n):
                y = squares_of(n)
                for kk in range(1, KT):
                    dve.wait_ge(squared, 8 * SPLIT[n] + kk + 1)
                    ins = TT(y[:, 0, 0:W[n]], y[:, 0, 0:W[n]], y[:, kk, 0:W[n]], ALU.add)
                    if kk < KT - 1:
                        order(ins)
                ins.then_inc(summed, 1)

            def take_in(first_o, n):
                for i in range(KT):
                    o = first_o + i
                    out_wait(o)
                    y = norm_source(n)[:, i, :]
                    if n == 2:
                        TT(y, y, pb[o % 4][:, 0:W[n]], ALU.add).then_inc(bank_free[o % 4], 1)
                    else:
                        CP(y, pb[o % 4][:, 0:W[n]]).then_inc(bank_free[o % 4], 1)
                    bank_freed(dve, o)
                    ins = TT(sq[:, i, 0:W[n]], y, y, ALU.mult)
                    if i == KT - 1:
                        ins.then_inc(last_squared, 1)
                    elif i:
                        order(ins)
                        ins = TT(sq[:, 0, 0:W[n]], sq[:, 0, 0:W[n]], sq[:, i, 0:W[n]], ALU.add)
                        if i == KT - 2:
                            ins.then_inc(summed, 1)
                        else:
                            order(ins)

            dve.wait_ge(vec_in, 16)
            for kk in range(KT):
                low_part(0, kk, "mem_norm", 0)
            add_squares(0)
            lb = vec[:, VEC_AT["lb"]:VEC_AT["lb"] + 4]
            TT(lb_m, lb, lb, ALU.subtract).then_inc(lb_shifted, 1)

            add_squares(1)

            def mem_out(i):
                o = MEM_O + i
                dve.wait_ge(rstd_ready, 1)
                out_wait(o)
                if i < 4:
                    ins = TT(mk[:, i, :], pb[o % 4][:, 0:ROWS], xrstd[:, 0:ROWS], ALU.mult)
                else:
                    at_i = P * (i // 2 * 2 - 4)
                    ins = TS(mv[:, i % 2, at_i:at_i + 2 * P], pb[o % 4][:, 0:2 * P], xrstd[:, ROWS + i % 2:ROWS + i % 2 + 1],
                             None, ALU.mult)
                ins.then_inc(bank_free[o % 4], 1)

            for i in range(2):
                mem_out(i)
            dve.wait_ge(rstd_ready, 2)
            for kk in range(KT):
                STT(tmp[:, kk, 0:ROWS], norm_source(1)[:, kk, :], vcol("norm_w", kk), rstd[:, 0:ROWS],
                    ALU.mult, ALU.mult).then_inc(scaled, 1)
            for kk in range(KT):
                dve.wait_ge(split_high, 8 + kk + 1)
                TT(xl[:, kk, 0:ROWS], tmp[:, kk, 0:ROWS], xh[:, kk, 0:ROWS].bitcast(f32), ALU.subtract).then_inc(split_low, 1)
            for i in range(2, 8):
                mem_out(i)
            dve.wait_ge(lb_exp, 1)
            order(nc.vector.reciprocal(lb_s, lb_e))
            order(TT(lb_e, lb_e, lb_s, ALU.mult))
            order(TT(lb_s, lb_e, lb_e, ALU.subtract))
            TS(lb_fl, lb_s, FLOOR, None, ALU.max)
            order(TS(lb_1m, lb_s, -1.0, 1.0, ALU.mult, ALU.add))
            dve.wait_ge(more_in, 10 * 16)
            TT(wba[:], wba[:], bc(vec[:, VEC_AT["gains"] + 16:VEC_AT["gains"] + 24], 2, 16), ALU.mult).then_inc(wba_scaled, 1)

            for step in FIRST:
                kind, i = step[0], step[-1]
                if kind == "lowrank":
                    bank, n = aux("lowrank")
                    aux_wait(dve, n)
                    CP(glr[:], bank[0:16, 0:ROWS]).then_inc(aux_free[n % 4], 1)
                if kind == "out":
                    o = IN_O + i
                    bank = pb[o % 4]
                    if i < 4:
                        bank_freed(dve, o)
                        TS(f[:, 4 + i, :], f[:, 4 + i, :], lb_1m[:, i:i + 1], lb_fl[:, i:i + 1], ALU.mult, ALU.add)
                        TS(k[:, 4 + i, :], k[:, 4 + i, :], lb_1m[:, i:i + 1], None, ALU.mult).then_inc(qk_ready, 1)
                        continue
                    if GATE <= i < V:
                        continue
                    out_wait(o)
                    if i < 8:
                        ins = CP(k[:, i - 4, :], bank[:, 0:ROWS])
                    elif i < 12:
                        ins = TS(q[:, i - 8, :], bank[:, 0:ROWS], SCALE, None, ALU.mult)
                    elif i < 16:
                        ins = CP(q[:, i - 8, :], bank[:, 0:ROWS])
                    elif i < GATE:
                        ins = CP(xq[:, i - XQ, :], bank[:, 0:ROWS])
                    else:
                        ins = CP(v[:, i % 2, P * (i // 2 * 2 - V):P * (i // 2 * 2 + 2 - V)], bank[:, 0:2 * P])
                    ins.then_inc(bank_free[o % 4], 1)
                if kind == "decay":
                    for x in range(2):
                        bank, n = aux("up", x)
                        aux_wait(dve, n)
                        for t in range(2):
                            ins = TS(f[:, 2 * x + t, :], bank[:, 256 * t:256 * t + 256], vcol("b_gate", 2 * x + t), None, ALU.add)
                        ins.then_inc(aux_free[n % 4], 1)
                        aux_freed(dve, n)
                    STT(tot[:, 0:4, :], f[:, 0:4, :], -1.0, f[:, 0:4, :], ALU.mult, ALU.max).then_inc(u_ready, 1)
                    dve.wait_ge(u_exp, 1)
                    STT(f[:, 0:4, :], f[:, 0:4, :], 0.0, tot[:, 0:4, :], ALU.min, ALU.subtract).then_inc(u_ready, 1)
                if kind == "level":
                    l, g = step[1], step[2]
                    heads = slice(4 * g, 4 * g + 4)
                    if l == 0 and g == 0:
                        dve.wait_ge(s_zero, 1)
                        dve.wait_ge(a_ready, 1)
                    if l < 8:
                        for x in range(2):
                            bank, n = aux("level", l, g, x)
                            aux_wait(dve, n)
                            nc.vector.copy_predicated(
                                s[:, 4 * g + 2 * x:4 * g + 2 * x + 2, :].rearrange("p h (b i) -> p (h b) i", b=2),
                                bc(masks[:, l, :], 1, 4), bank[:, :].rearrange("p (m i) -> p m i", m=4))\
                                .then_inc(aux_free[n % 4], 1)
                    else:
                        bank, n = aux("level", l, g, 0)
                        aux_wait(dve, n)
                        CP(s3[:, heads, :], bank[:, :].rearrange("p (h i) -> p h i", h=4)).then_inc(aux_free[n % 4], 1)
                    if l == 0:
                        TT(q[:, heads, :], q[:, heads, :], f[:, heads, :], ALU.mult).then_inc(level_up[g], 1)
                    elif l < 8:
                        b = 2 ** (l - 1)
                        m = 128 // b
                        now = f[:, heads, :] if l == 1 else tot[:, heads, TOT[l]:TOT[l] + 2 * m]
                        now = now.rearrange("p h (m two) -> p h m two", two=2)
                        dve.wait_ge(level_up[g], l)
                        for hd in range(4):
                            qv = q[:, 4 * g + hd, :].rearrange("p (m two b) -> p m two b", two=2, b=b)
                            kv = k[:, 4 * g + hd, :].rearrange("p (m two b) -> p m two b", two=2, b=b)
                            TT(qv[:, :, 1, :], qv[:, :, 1, :], bc(now[:, hd, :, 0], 2, b), ALU.mult)
                            ins = TT(kv[:, :, 0, :], kv[:, :, 0, :], bc(now[:, hd, :, 1], 2, b), ALU.mult)
                        if l < 7:
                            ins = TT(tot[:, heads, TOT[l + 1]:TOT[l + 1] + m], now[:, :, :, 0], now[:, :, :, 1], ALU.mult)
                        ins.then_inc(level_up[g], 1)
                if kind == "scores":
                    bank, n = aux("scores", i)
                    cols = slice(2 * i, 2 * i + 2)
                    aux_wait(dve, n)
                    order(nc.vector.reduce_max(mx[:, cols], bank[:, :].rearrange("p (e m) -> p e m", e=2), AX.X))
                    TS(nmx[:, cols], mx[:, cols], -SCALE, None, ALU.mult).then_inc(max_ready, 1)
                if kind == "weights":
                    cols = slice(2 * i, 2 * i + 2)
                    aux_freed(dve, AUX[("scores", i)])
                    order(nc.vector.reciprocal(ri[:, cols], rs[:, cols]))
                    for e in range(2):
                        ins = TS(prob[:, i % 2, e, :], prob[:, i % 2, e, :], ri[:, 2 * i + e:2 * i + e + 1], None, ALU.mult)
                    ins.then_inc(prob_ready, 1)
                if kind == "probs":
                    bank, n = aux("probs", i)
                    aux_wait(dve, n)
                    CP(pt[:, 2 * (i % 2):2 * (i % 2) + 2, :, P * (i // 2):P * (i // 2) + P],
                       bank[:, :].rearrange("p (e m s) -> p e m s", e=2, m=2)).then_inc(aux_free[n % 4], 1)
                if kind == "o":
                    bank, n = aux("o", i)
                    if i >= 4:
                        dve.wait_ge(mix_high, i - 3)
                    aux_wait(dve, n)
                    CP(ot[:, i % 4].rearrange("p e r -> p (e r)"), bank[:, :]).then_inc(aux_free[n % 4], 1)
                if kind == "o_norm":
                    dve.wait_ge(o_rstd, i + 1)
                    for e in range(2):
                        wv = vcol("gla_norm", e) if i < 4 else vcol("hgrn_norm" if i < 6 else "xattn_norm")
                        r = rstd[:, 0:ROWS] if i < 4 else rstd[:, ROWS * e:ROWS * e + ROWS]
                        ins = STT(ot[:, i % 4, e, :], ot[:, i % 4, e, :], wv, r, ALU.mult, ALU.mult)
                    order(ins)
                    TT(ot[:, i % 4], ot[:, i % 4], gate[:, 2 * i:2 * i + 2, :], ALU.mult).then_inc(o_mixed, 1)
                if kind == "o_split":
                    dve.wait_ge(mix_high, i + 1)
                    TT(mixl[:, 2 * i:2 * i + 2, :], ot[:, i % 4], mixh[:, 2 * i:2 * i + 2, :].bitcast(f32),
                       ALU.subtract).then_inc(mix_low, 1)
            take_in(WOUT_O, 2)
            dve.wait_ge(rstd_ready, 3)
            for t in range(KT + 1):
                if t < KT:
                    STT(h[:, t, META:LEN], h[:, t, META:LEN], vcol("final", t), rstd[:, 0:ROWS], ALU.mult, ALU.mult)\
                        .then_inc(h_ready, 1)
                if t:
                    low_part(3, t - 1, "gains", 0)

            def up_loop(layer, first_o, w):
                dve.wait_ge(rstd_ready, 4 + 4 * layer)
                with dve.Fori(0, UP // 4) as g:
                    for pair in range(2):
                        done = layer * FT + pair
                        tile = dve.snap(g * 2 + pair)
                        dve.wait_ge(passed, g * 4 + OUT_PASS[first_o + 2 * pair])
                        TT(sil[:, pair, 0:w], pb[2 * pair][:, 0:w], xrstd[:, 0:w], ALU.mult)\
                            .then_inc(bank_free[2 * pair], 1)
                        dve.wait_ge(passed, g * 4 + OUT_PASS[first_o + 2 * pair + 1])
                        TT(hid[:, pair, 0:w], pb[2 * pair + 1][:, 0:w], xrstd[:, 0:w], ALU.mult)\
                            .then_inc(bank_free[2 * pair + 1], 1)
                        dve.wait_ge(bank_free[2 * pair + 1], g + (first_o // 4 + 1))
                        dve.wait_ge(sil_ready, g * 2 + (done + 1))
                        TT(hid[:, pair, 0:w], hid[:, pair, 0:w], sil[:, pair, 0:w], ALU.mult).then_inc(hid_ready, 1)
                        dve.wait_ge(hid_high, g * 2 + (done + 1))
                        TT(hl[:, bass.ds(tile, 1), 0:w].rearrange("p a s -> p (a s)"), hid[:, pair, 0:w],
                           hh[:, bass.ds(tile, 1), 0:w].rearrange("p a s -> p (a s)").bitcast(f32),
                           ALU.subtract).then_inc(hid_low, 1)

            up_loop(0, UP1_O, LEN)
            take_in(DOWN1_O, 4)
            combine(4, 8, 0.5, 5)

            def part_of_a(level, u):
                if level == 0 and u >= 2:
                    aux_wait(dve, AUX[("x17", u - 2)])
                if level == 1:
                    aux_wait(dve, AUX[("x17", 6 + u)] if u < 2 else AUX[("x34", u - 2)])
                if level == 0 and u == 0:
                    dve.wait_ge(am_ready, 8)
                TT(aoff[:, u % 2], am[:, u], bc(lvl[:, level, :], 1, 4), ALU.mult).then_inc(aoff_ready, 1)

            def conv_tile(pos):
                if pos < 12:
                    TS(qkv[:, pos, :], pre[:, pos, :], vcol("dconv", 12 + pos), None, ALU.mult).then_inc(tap1, 1)
                t = pos - 1
                if 0 <= t < 12:
                    dve.wait_ge(tap1, t + 1)
                    STT(qkv[:, t, 1:LEN], pre[:, t, 0:LEN - 1], vcol("dconv", t), qkv[:, t, 1:LEN], ALU.mult, ALU.add)\
                        .then_inc(tap2, 1)
                t = pos - 2
                if 0 <= t < 12:
                    dve.wait_ge(tap2, t + 1)
                    STT(qkv[:, t, 0:LEN - 1], pre[:, t, 1:LEN], vcol("dconv", 24 + t), qkv[:, t, 0:LEN - 1],
                        ALU.mult, ALU.add).then_inc(conv_done, 1)

            for step in MIXER:
                kind, i = step[0], step[-1]
                if step in MIX_OUT:
                    o, p, half = MIX_OUT[step]
                    bank = pb[o % 4]
                if kind == "logits":
                    bank, n = aux("ba")
                    aux_wait(dve, n)
                    TT(ba[:], bank[0:16, 0:LEN], xrstd[0:16, :], ALU.mult).then_inc(aux_free[n % 4], 1)
                    bank, n = aux("logits")
                    aux_wait(dve, n)
                    TT(logit_a, bank[0:CH, 0:64].rearrange("p (c e) -> p c e", c=NC)[:, :, 8:16],
                       bc(vec[0:CH, VEC_AT["dt_bias"]:VEC_AT["dt_bias"] + 8], 1, NC), ALU.add).then_inc(a_logit, 1)
                    dve.wait_ge(a_logit, 1)
                    STT(abs_a, logit_a, -1.0, logit_a, ALU.mult, ALU.max).then_inc(a_logit, 1)
                    dve.wait_ge(a_soft, 1)
                    order(STT(grate, logit_a, 0.0, abs_a, ALU.max, ALU.add))
                    STT(grate, grate, -1.0, bc(ea, 1, NC), ALU.mult, ALU.mult).then_inc(g_ready, 1)
                if kind == "cumulate":
                    bank, n = aux("cumulate")
                    aux_wait(dve, n)
                    CP(small2[0:CH, 136:200], bank[0:CH, 0:64]).then_inc(aux_free[n % 4], 1)
                    aux_freed(dve, n)
                    for d in range(2):
                        ins = TT(ed[:, d], gtot[:, :, d, :], gc[:, d], ALU.subtract)
                    ins.then_inc(td_ready, 1)
                    dve.wait_ge(ec_ready, 1)
                    order(TS(small2[0:CH, 200:232], small2[0:CH, 200:232], -1.0, None, ALU.mult))
                if kind == "qkv":
                    out_wait(o)
                    if i == 0:
                        dve.wait_ge(rstd_ready, 6)
                    TT(pre[:, i, :], bank[:, 0:LEN], xrstd[:], ALU.mult).then_inc(bank_free[o % 4], 1)
                    bank_freed(dve, o)
                    conv_tile(i)
                if step == ("z", 0):
                    conv_tile(12)
                    conv_tile(13)
                if kind == "l2norm":
                    dve.wait_ge(l2_rstd, 1)
                    STT(qn, qn, SCALE, sq[:, 0:4, :], ALU.mult, ALU.mult).then_inc(qk_normed, 1)
                    TT(kn, kn, sq[:, 4:8, :], ALU.mult).then_inc(qk_normed, 1)
                if kind == "chunk":
                    if i:
                        aux_freed(dve, AUX[("qk", i - 1)])
                    for d in range(2):
                        bank, n = aux(f"row{d}", i)
                        dve.wait_ge(row_exp, 2 * i + d + 1)
                        TT(dmat[:, d, 0], bc(gc[:, d, i, :], 2, CH), bank[0:CH, 0:4 * CH].rearrange("p (h t) -> p h t", h=4),
                           ALU.subtract).then_inc(aux_free[n % 4], 1)
                        aux_freed(dve, n)
                        if d == 0:
                            order(TS(dmat[:, d, 1], dmat[:, d, 0], 0.0, None, ALU.min))
                        TS(dmat[:, d, 0], dmat[:, d, 0], 0.0, None, ALU.max).then_inc(diff_ready, 1)
                    bkk, nkk = aux("kk", i)
                    bqk, nqk = aux("qk", i)
                    aux_wait(dve, nqk)
                    for d in range(2):
                        dve.wait_ge(decay_ready, 2 * i + d + 1)
                        ins = TT(am[:, 2 * i + d], dmat[:, d, 1 - d], bkk[0:CH, 0:4 * CH].rearrange("p (h t) -> p h t", h=4),
                                 ALU.mult)
                        ins.then_inc(aux_free[nkk % 4] if d else am_raw, 1)
                    for d in range(2):
                        ins = TT(att[:, 2 * i + d], dmat[:, d, 0], bqk[0:CH, 0:4 * CH].rearrange("p (h t) -> p h t", h=4),
                                 ALU.mult)
                        ins.then_inc(aux_free[nqk % 4] if d else att_raw, 1)
                if kind == "invert":
                    CP(tb[:], eye17[:])
                    dve.wait_ge(blocks_in, 80)
                    order(TS(bn[:], bn[:], -1.0, None, ALU.mult))
                    for r in range(1, SUB):
                        prod = pr[:, 0:r * r].rearrange("p (c j) -> p c j", c=r)
                        order(TT(prod, bc(bn[:, r, 0:r], 1, r), tb[:, 0:r, 0:r].rearrange("p j c -> p c j"), ALU.mult))
                        ins = nc.vector.tensor_reduce(tb[:, r, 0:r], prod, AX.X, ALU.add)
                        if r < SUB - 1:
                            order(ins)
                    ins.then_inc(inverse_ready, 1)
                if kind == "fourier_in":
                    out_wait(o)
                    TT(fu[:, i, :], bank[:, 0:LEN], xrstd[:], ALU.mult).then_inc(bank_free[o % 4], 1)
                if kind == "z":
                    out_wait(o)
                    TT(zs[:, i, :], bank[:, 0:ROWS], xrstd[:, META:LEN], ALU.mult).then_inc(bank_free[o % 4], 1)
                if kind == "gate":
                    g = 8 * step[1] + i
                    if g >= 2:
                        bank_freed(dve, MIX_OUT[("branch", (g - 2) // 8, (g - 2) % 8)][0])
                    if g >= 10:
                        dve.wait_ge(mg_ready, g - 9)
                    out_wait(o)
                    TT(gt[:, g % 2, :], bank[:, 0:ROWS], xrstd[:, META:LEN], ALU.mult).then_inc(bank_free[o % 4], 1)
                if kind == "dft":
                    if i == 0:
                        dve.wait_ge(h_saved, 16)
                    for x in range(2):
                        bank, n = aux("dft_in", i, x)
                        aux_wait(dve, n)
                        CP(pf[:, i % 2, 2 * x:2 * x + 2, :].rearrange("p c f -> p (c f)"), bank[0:CH, :])\
                            .then_inc(aux_free[n % 4], 1)
                    bank, n = aux("dft_out", i)
                    dve.wait_ge(y_high, i + 1)
                    TT(yl[:, i, :], bank[:, 0:ROWS], yh[:, i, :].bitcast(f32), ALU.subtract).then_inc(aux_free[n % 4], 1)
                if kind == "branch":
                    g = 8 * step[1] + i
                    out_wait(o)
                    dve.wait_ge(gate_ready, g + 1)
                    if step[1] == 0:
                        TT(mg[:, i, :], bank[:, 0:ROWS], gt[:, g % 2, :], ALU.mult).then_inc(bank_free[o % 4], 1)
                    else:
                        if i == 0 and step[1] == 1:
                            for t in range(4, 8):
                                bank_freed(dve, MIX_OUT[("branch", 0, t)][0])
                        if step[1] == 2:
                            dve.wait_ge(mg_ready, i + 1)
                        TT(gt[:, g % 2, :], bank[:, 0:ROWS], gt[:, g % 2, :], ALU.mult).then_inc(bank_free[o % 4], 1)
                        bank_freed(dve, o)
                        TT(mg[:, i, :], mg[:, i, :], gt[:, g % 2, :], ALU.add).then_inc(mg_ready, 1)
                if kind == "sconv":
                    t, j = step[1], step[2]
                    out_wait(o)
                    TT(sc[:, t % 2, j, :], bank[:, 0:LEN], xrstd[:], ALU.mult).then_inc(bank_free[o % 4], 1)
                    if j == 2:
                        bank_freed(dve, o)
                        bank_freed(dve, o - 1)
                        bank_freed(dve, o - 2)
                        m, y = cc[:, t % 2, 0, :], cc[:, t % 2, 1, 0:ROWS]
                        order(TT(m, sc[:, t % 2, 1, :], sc[:, t % 2, 2, :], ALU.mult))
                        order(TS(y, m[:, META:LEN], vcol("sconv", 4 + t), None, ALU.mult))
                        order(STT(y, m[:, META - 1:LEN - 1], vcol("sconv", t), y, ALU.mult, ALU.add))
                        order(STT(y[:, 0:ROWS - 1], m[:, META + 1:LEN], vcol("sconv", 8 + t), y[:, 0:ROWS - 1], ALU.mult, ALU.add))
                        TT(y, y, sc[:, t % 2, 0, META:LEN], ALU.mult).then_inc(yc_ready, 1)
                        dve.wait_ge(y_high, 4 + t + 1)
                        TT(yl[:, t, :], y, yh[:, t, :].bitcast(f32), ALU.subtract).then_inc(y_low, 1)
                if kind == "u0":
                    part_of_a(0, i)
                if step == ("u17", 7):
                    part_of_a(1, 0)
                if kind == "x34" and i < 7:
                    part_of_a(1, i + 1)
                if kind == "t17":
                    bank, n = aux("t17", i)
                    aux_wait(dve, n)
                    TT(tm[:, i], tm[:, i], bank[0:CH, 0:4 * CH].rearrange("p (h t) -> p h t", h=4), ALU.subtract)\
                        .then_inc(aux_free[n % 4], 1)
                if kind == "t34":
                    bank, n = aux("t34", i)
                    aux_wait(dve, n)
                    m = tm if i % 2 else um
                    TT(m[:, i], m[:, i], bank[0:CH, 0:4 * CH].rearrange("p (h t) -> p h t", h=4), ALU.subtract)\
                        .then_inc(aux_free[n % 4], 1)
                    if i % 2 == 0:
                        aux_freed(dve, n)
                        TT(um[:, i], um[:, i], bc(beta[:, i // 2, 0:4], 2, CH), ALU.mult).then_inc(um_ready, 1)
                if kind in ("ks", "vn", "od", "su"):
                    chunk = (i, NC - 1 - i)
                    if kind == "ks":
                        for d in range(2):
                            bank, n = aux("ks", i, d)
                            aux_wait(dve, n)
                            for hd in range(4):
                                ins = STT(rr[:, d, hd, :], bank[0:CH, P * hd:P * hd + P], nec[:, d, chunk[d], hd:hd + 1],
                                          vt[:, chunk[d], hd, :], ALU.mult, ALU.add)
                            ins.then_inc(aux_free[n % 4], 1)
                    if kind == "vn":
                        bank, n = aux("vn", i, 1)
                        aux_wait(dve, n)
                        if 0 < i < NC - 1:
                            dve.wait_ge(vdec_ready, 2 * i)
                        TT(vnew[:, 1], bank[0:CH, :].rearrange("p (h d) -> p h d", h=4), bc(beta[:, chunk[1], 4:8], 2, P),
                           ALU.mult).then_inc(aux_free[n % 4], 1)
                    for d in range(2) if kind == "od" else ():
                        bank, n = aux("od", i, d)
                        c0 = CH * chunk[d]
                        part = bank[:, 0:4 * CH].rearrange("p (h t) -> p h t", h=4)
                        aux_wait(dve, n)
                        if i < 2:
                            ins = CP(od[:, :, c0:c0 + CH], part)
                        else:
                            ins = TT(od[:, :, c0:c0 + CH], od[:, :, c0:c0 + CH], part, ALU.add)
                        ins.then_inc(aux_free[n % 4], 1)
                        aux_freed(dve, n)
                    if kind == "su":
                        for d in range(2):
                            bank, n = aux("su", i, d)
                            aux_wait(dve, n)
                            for hd in range(4):
                                b_ = bank[:, P * hd:P * hd + P]
                                if i == 0:
                                    ins = CP(state[:, d, hd, :], b_)
                                else:
                                    ins = STT(state[:, d, hd, :], state[:, d, hd, :], elast[:, 2 * chunk[d] + d, hd:hd + 1],
                                              b_, ALU.mult, ALU.add)
                            ins.then_inc(aux_free[n % 4], 1)
                            aux_freed(dve, n)
                if kind == "delta_norm":
                    for e in range(2):
                        dve.wait_ge(drs_ready, e + 1)
                        both = slice(2 * e, 2 * e + 2)
                        order(STT(yd[:, both, :], od[:, both, META:LEN], vcol("dn_norm"),
                                  drs[:].rearrange("p (h t) -> p h t", h=2), ALU.mult, ALU.mult))
                        TT(yd[:, both, :], yd[:, both, :], zs[:, both, :], ALU.mult).then_inc(yd_ready, 1)
                    for e in range(4):
                        dve.wait_ge(y_high, 8 + e + 1)
                        TT(yl[:, e, :], yd[:, e, :], yh[:, e, :].bitcast(f32), ALU.subtract).then_inc(y_low, 1)
            for kk in range(KT):
                dve.wait_ge(mg_high, kk + 1)
                TT(xl[:, kk, 0:ROWS], mg[:, kk, :], xh[:, kk, 0:ROWS].bitcast(f32), ALU.subtract).then_inc(mg_low, 1)
            take_in(OUT2_O, 6)
            dve.wait_ge(h_back, 16)
            combine(6, 24, 1.0, 7)
            up_loop(1, UP2_O, ROWS)
            take_in(DOWN2_O, 8)
            combine(8, 40, 0.5)

        @block.tensor
        def _(pe):
            M = nc.tensor.matmul

            def norm_stat(n):
                bank, use = aux("stat", n)
                y = squares_of(n)
                late = n in (2, 4, 6, 8)
                aux_open(use)
                pe.wait_ge(summed, n + 1)
                ins = M(bank[:, 0:W[n]], ones[:], y[:, 0, 0:W[n]], start=True, stop=not late)
                if late:
                    pe.wait_ge(last_squared, n // 2)
                    ins = M(bank[:, 0:W[n]], ones[:], y[:, KT - 1, 0:W[n]], start=False, stop=True)
                if n == 0:
                    for rt in range(2):
                        ins = M(bank[:, ROWS + rt:ROWS + rt + 1], y[:, 0, P * rt:P * rt + P], ones[:, 0:1], start=True, stop=True)
                ins.then_inc(aux_full, 1)

            def products(bank, slot, pairs, hi_, lo_, c0, w, first, last, each=None):
                for m, (t, kk) in enumerate(pairs):
                    if each is not None:
                        each(kk)
                    for n, (wt, x) in enumerate(((whi, hi_), (whi, lo_), (wlo, hi_))):
                        ins = M(bank[:, 0:w], wt[:, slot, P * t:P * t + P], x[:, kk, c0:c0 + w],
                                start=first and m == 0 and n == 0, stop=last and m == len(pairs) - 1 and n == 2)
                return ins

            def tiles_split(n):
                return lambda kk: pe.wait_ge(split_low, 8 * SPLIT[n] + kk + 1)

            def open_output(o, p):
                pe.wait_ge(lo_ready, p + 1)
                if o >= 4:
                    pe.wait_ge(bank_free[o % 4], o // 4)

            def output(o, p, hi_, lo_, w, c0=0, tiles=KT, half=0, each=None):
                open_output(o, p)
                pairs = [(tiles * half + t, t) for t in range(tiles)]
                products(pb[o % 4], p % RING, pairs, hi_, lo_, c0, w, True, True, each).then_inc(passed, 1)

            def output_rows(o, p, hi_, lo_):
                if p % 2:
                    return
                open_output(o, p)
                open_output(o + 1, p + 1)
                r = p % RING
                for rt in range(2):
                    for kk in range(KT):
                        for n, (wt, x) in enumerate(((whi, hi_), (whi, lo_), (wlo, hi_))):
                            ins = M(pb[(o + rt) % 4][:, 0:2 * P], x[:, kk, P * rt:P * rt + P],
                                    wt[:, r:r + 2, P * kk:P * kk + P], start=kk == 0 and n == 0, stop=kk == KT - 1 and n == 2)
                ins.then_inc(passed, 2)

            def transposes(bank, src, rows):
                for hd in range(4):
                    w_ = src[hd].partition_size()
                    ins = nc.tensor.transpose(bank[0:rows, w_ * hd:w_ * hd + w_], src[hd], ident[0:w_, 0:w_])
                return ins

            def w_out(k):
                i, half = W_OUT[k]
                o, p = WOUT_O + i, WOUT_P + k
                pe.wait_ge(lo_ready, p + 1)
                if half == 0:
                    pe.wait_ge(bank_free[o % 4], o // 4)
                products(pb[o % 4], p % RING, [(t, 8 * half + t) for t in range(8)], mixh, mixl, 0, ROWS,
                         half == 0, half == 1).then_inc(passed, 1)

            pe.wait_ge(ones_in, 16)
            for i in range(8):
                if i < 4:
                    output(MEM_O + i, MEM_P + i, memh, meml, ROWS, each=tiles_split(0) if i == 0 else None)
                    if i < 2:
                        norm_stat(i)
                else:
                    output_rows(MEM_O + i, MEM_P + i, memh, meml)
            pe.wait_ge(more_in, 10 * 16)
            pe.wait_ge(split_low, 16)
            for step in FIRST:
                kind, i = step[0], step[-1]
                if kind == "lowrank":
                    bank, n = aux("lowrank")
                    aux_open(n)
                    for kk in range(KT):
                        ins = M(bank[0:16, 0:ROWS], wglr[:, kk, :], tmp[:, kk, 0:ROWS], start=kk == 0, stop=kk == KT - 1)
                    ins.then_inc(aux_full, 1)
                if kind == "out":
                    (output_rows if i >= V else lambda *x: output(*x, ROWS))(IN_O + i, IN_P + i, xh, xl)
                if kind == "decay":
                    aux_freed(pe, AUX[("lowrank",)])
                    for x in range(2):
                        bank, n = aux("up", x)
                        aux_open(n)
                        for t in range(2):
                            ins = M(bank[:, 256 * t:256 * t + 256], upw[:, P * (2 * x + t):P * (2 * x + t) + P], glr[:],
                                    start=True, stop=True)
                        ins.then_inc(aux_full, 1)
                if kind == "level":
                    l, g = step[1], step[2]
                    if l == 0:
                        for o in (range(IN_O + 4, IN_O + 16) if g == 0 else ()):
                            bank_freed(pe, o)
                        pe.wait_ge(qk_ready, 4)
                    else:
                        pe.wait_ge(level_up[g], l)
                    for x in range(2):
                        if l == 8 and x:
                            break
                        bank, n = aux("level", l, g, x)
                        aux_open(n)
                        for m in range(4):
                            if l < 8:
                                hd, blk = 4 * g + 2 * x + m // 2, slice(P * (m % 2), P * (m % 2) + P)
                                ins = M(bank[:, P * m:P * m + P], k[:, hd, blk], q[:, hd, blk], start=True, stop=True)
                            else:
                                ins = M(bank[:, P * m:P * m + P], k[:, 4 * g + m, 0:P], q[:, 4 * g + m, P:ROWS], start=True, stop=True)
                        ins.then_inc(aux_full, 1)
                if kind == "wout":
                    if i == 0:
                        pe.wait_ge(mix_low, 4)
                    w_out(i)
                if kind == "scores":
                    st, pair = i // 2, i % 2
                    bank, n = aux("scores", i)
                    aux_open(n)
                    if i == 0:
                        for o in list(range(4)) + list(range(IN_O + XQ, IN_O + XQ + 4)):
                            bank_freed(pe, o)
                    for e in range(2):
                        ins = M(bank[:, ROWS * e:ROWS * e + ROWS], xq[:, 2 * pair + e, P * st:P * st + P], mk[:, 2 * pair + e, :],
                                start=True, stop=True)
                    ins.then_inc(aux_full, 1)
                if kind == "probs":
                    bank, n = aux("probs", i)
                    aux_open(n)
                    pe.wait_ge(prob_ready, i + 1)
                    transposes(bank, [prob[:, i % 2, m // 2, P * (m % 2):P * (m % 2) + P] for m in range(4)], P)\
                        .then_inc(aux_full, 1)
                if kind == "o":
                    bank, n = aux("o", i)
                    aux_open(n)
                    if i == 0:
                        for g in range(2):
                            for l in (6, 7, 8):
                                for x in range(2 if l < 8 else 1):
                                    aux_freed(pe, AUX[("level", l, g, x)])
                    if i == 6:
                        for u in range(4):
                            aux_freed(pe, AUX[("probs", u)])
                        for o in range(4, 8):
                            bank_freed(pe, o)
                    if i < 6:
                        bank_freed(pe, IN_O + V + 2 * i)
                        bank_freed(pe, IN_O + V + 2 * i + 1)
                    for e in range(2):
                        if i < 6:
                            hd = i if i < 4 else 2 * i - 4 + e
                            col = P * (2 * i + e)
                            M(bank[:, ROWS * e:ROWS * e + P], v[:, 0, col:col + P], s[:, hd, 0:P], start=True, stop=True)
                            M(bank[:, ROWS * e + P:ROWS * e + ROWS], v[:, 0, col:col + P], s3[:, hd, :], start=True, stop=False)
                            ins = M(bank[:, ROWS * e + P:ROWS * e + ROWS], v[:, 1, col:col + P], s[:, hd, P:ROWS],
                                    start=False, stop=True)
                        else:
                            hd = 2 * (i - 6) + e
                            for mt in range(2):
                                ins = M(bank[:, ROWS * e:ROWS * e + ROWS], mv[:, mt, P * hd:P * hd + P], pt[:, hd, mt, :],
                                        start=mt == 0, stop=mt == 1)
                    ins.then_inc(aux_full, 1)
                if kind == "o_norm":
                    bank, n = aux("o_norm", i)
                    aux_open(n)
                    pe.wait_ge(o_squared, i + 1)
                    for e in range(2):
                        if i < 4:
                            ins = M(bank[:, 0:ROWS], ones[:], sqo[:, i % 4, e, :], start=e == 0, stop=e == 1)
                        else:
                            ins = M(bank[:, ROWS * e:ROWS * e + ROWS], ones[:], sqo[:, i % 4, e, :], start=True, stop=True)
                    ins.then_inc(aux_full, 1)
            pe.wait_ge(mix_low, 8)
            for m in range(4, 16):
                w_out(m)
            norm_stat(2)

            def up_loop(first_o, first_p, w, norm):
                output(first_o, first_p, xh, xl, w, each=tiles_split(norm))
                norm_stat(norm)
                for n in range(1, 4):
                    output(first_o + n, first_p + n, xh, xl, w)
                with pe.Fori(0, UP // 4 - 1) as g:
                    for n in range(4):
                        pe.wait_ge(lo_ready, g * 4 + (first_p + 4 + n + 1))
                        pe.wait_ge(bank_free[n], g + (first_o // 4 + 1))
                        products(pb[n], n, [(t, t) for t in range(KT)], xh, xl, 0, w, True, True).then_inc(passed, 1)

            def down_loop(layer, first_o, first_p, w):
                pe.wait_ge(hid_low, FT * layer + FT - 2)
                with pe.Fori(0, 2) as g:
                    for n in range(12):
                        part = n % 3
                        pe.wait_ge(lo_ready, g * 12 + (first_p + n + 1))
                        if part == 0:
                            pe.wait_ge(bank_free[n // 3], g + first_o // 4)
                        if n == 2:
                            pe.wait_ge(hid_low, FT * layer + FT)
                        k0, size = (0, 8, 15)[part], (8, 7, 7)[part]
                        products(pb[n // 3], n % RING, [(t, k0 + t) for t in range(size)], hh, hl, 0, w,
                                 part == 0, part == 2).then_inc(passed, 1)

            up_loop(UP1_O, UP1_P, LEN, 3)
            down_loop(0, DOWN1_O, DOWN1_P, LEN)
            norm_stat(4)

            for step in MIXER:
                kind, i = step[0], step[-1]
                if step in MIX_OUT:
                    o, p, half = MIX_OUT[step]
                if kind == "logits":
                    bank, n = aux("ba")
                    aux_open(n)
                    pe.wait_ge(wba_scaled, 1)
                    for kk in range(KT):
                        ins = M(bank[0:16, 0:LEN], wba[:, kk, :], h[:, kk, :], start=kk == 0, stop=kk == KT - 1)
                    ins.then_inc(aux_full, 1)
                    aux_freed(pe, n)
                    bank, n = aux("logits")
                    aux_open(n)
                    for c in range(NC):
                        ins = nc.tensor.transpose(bank[0:CH, 16 * c:16 * c + 16], ba[:, CH * c:CH * c + CH], ident[0:16, 0:16])
                    ins.then_inc(aux_full, 1)
                if kind == "cumulate":
                    bank, n = aux("cumulate")
                    aux_open(n)
                    pe.wait_ge(g_ready, 1)
                    for d in range(2):
                        M(bank[0:CH, 16 * d:16 * d + 16], tri[:, d, :], grate[:, :, 4 * d:4 * d + 4], start=True, stop=True)
                    M(bank[0:CH, 32:64], ones[0:CH, 0:CH], small2[0:CH, 96:128], start=True, stop=True).then_inc(aux_full, 1)
                if kind in ("qkv", "fourier_in", "sconv"):
                    output(o, p, xh, xl, LEN, each=tiles_split(5) if step == ("qkv", 0) else None)
                    if step == ("qkv", 0):
                        norm_stat(5)
                if kind in ("z", "gate"):
                    output(o, p, xh, xl, ROWS, META)
                if kind == "branch":
                    if i == 0:
                        pe.wait_ge(y_low, 4 * step[1]) if step[1] else aux_freed(pe, AUX[("dft_out", 3)])
                    output(o, p, yh, yl, ROWS, 0, 4, half)
                if kind == "l2norm":
                    for t in range(8):
                        bank, n = aux("l2", t)
                        aux_open(n)
                        pe.wait_ge(qk_squared, t // 4 + 1)
                        M(bank[:, 0:LEN], ones[:], sq[:, t, :], start=True, stop=True).then_inc(aux_full, 1)
                if kind == "chunk":
                    rows = slice(CH * i, CH * i + CH)
                    if i == 0:
                        pe.wait_ge(qk_normed, 2)
                        pe.wait_ge(silu_qkv, 3)
                    for use, src in (("kt", kn), ("vt", vf)):
                        bank, n = aux(use, i)
                        aux_open(n)
                        for hd in range(4):
                            ins = nc.tensor.transpose(bank[0:CH, P * hd:P * hd + P], src[:, hd, rows], ident[:])
                        ins.then_inc(aux_full, 1)
                    for d in range(2):
                        bank, n = aux(f"row{d}", i)
                        aux_open(n)
                        for hd in range(4):
                            ins = M(bank[:, CH * hd:CH * hd + CH], grate[:, i, 4 * d + hd:4 * d + hd + 1].to_broadcast([CH, P]),
                                    tri[:, d, :], start=True, stop=True)
                        ins.then_inc(aux_full, 1)
                    for use, other in (("kk", kn), ("qk", qn)):
                        bank, n = aux(use, i)
                        aux_open(n)
                        for hd in range(4):
                            ins = M(bank[0:CH, CH * hd:CH * hd + CH], kn[:, hd, rows], other[:, hd, rows], start=True, stop=True)
                        ins.then_inc(aux_full, 1)
                if kind == "dft":
                    if i == 0:
                        pe.wait_ge(late_in, 16)
                        bank_freed(pe, MIX_OUT[("fourier_in", 3)][0])
                    for x in range(2):
                        bank, n = aux("dft_in", i, x)
                        aux_open(n)
                        if i == 0:
                            for t in range(4):
                                bank_freed(pe, MIX_OUT[("fourier_in", t)][0])
                        for e in range(2):
                            c = 2 * x + e
                            ins = M(bank[0:CH, 256 * e:256 * e + 256], fu[:, i, CH * c:CH * c + CH], fmat[:], start=True, stop=True)
                        ins.then_inc(aux_full, 1)
                    bank, n = aux("dft_out", i)
                    aux_open(n)
                    for x in range(2):
                        aux_freed(pe, AUX[("dft_in", i, x)])
                        for m in range(4):
                            c, cs = 2 * x + m // 2, m % 2
                            ins = M(bank[:, 0:ROWS], pf[:, i % 2, c, P * cs:P * cs + P], cmat[:, c, cs, :],
                                    start=x == 0 and m == 0, stop=x == 1 and m == 3)
                    ins.then_inc(aux_full, 1)
                if kind in ("u0", "u17"):
                    if step == ("u0", 0):
                        pe.wait_ge(blocks_out, 80)
                    bank, n = aux(kind, i)
                    aux_open(n)
                    if kind == "u17":
                        aux_freed(pe, AUX[("t17", i)])
                    transposes(bank, [tm[:, i, hd, :] for hd in range(4)], CH).then_inc(aux_full, 1)
                if kind in ("x17", "x34"):
                    bank, n = aux(kind, i)
                    aux_open(n)
                    aux_freed(pe, AUX[("u0" if kind == "x17" else "u17", i)])
                    pe.wait_ge(aoff_ready, (0 if kind == "x17" else 8) + i + 1)
                    for hd in range(4):
                        ins = M(bank[0:CH, CH * hd:CH * hd + CH], aoff[:, i % 2, hd, :], um[:, i, hd, :], start=True, stop=True)
                    ins.then_inc(aux_full, 1)
                if kind in ("t17", "t34"):
                    bank, n = aux(kind, i)
                    aux_open(n)
                    aux_freed(pe, AUX[("x" + kind[1:], i)])
                    flip = kind == "t34" and i % 2 == 0
                    for hd in range(4):
                        l_, r_ = (tm[:, i, hd, :], xm[:, i % 2, hd, :]) if flip else (xm[:, i % 2, hd, :], tm[:, i, hd, :])
                        ins = M(bank[0:CH, CH * hd:CH * hd + CH], l_, r_, start=True, stop=True)
                    ins.then_inc(aux_full, 1)
                if kind in ("ks", "vn", "od", "su"):
                    chunk = (i, NC - 1 - i)
                    if step == ("vn", 0):
                        pe.wait_ge(um_ready, 4)
                        for u in (1, 3, 5, 7):
                            aux_freed(pe, AUX[("t34", u)])
                        for c in range(NC):
                            aux_freed(pe, AUX[("kt", c)])
                            aux_freed(pe, AUX[("vt", c)])
                        pe.wait_ge(att_ready, 8)
                        pe.wait_ge(qe_ready, 8)
                    if kind == "ks":
                        for d in range(2):
                            bank, n = aux("ks", i, d)
                            aux_open(n)
                            aux_freed(pe, AUX[("su", i - 1, d)])
                            for hd in range(4):
                                ins = M(bank[0:CH, P * hd:P * hd + P], kn[:, hd, CH * chunk[d]:CH * chunk[d] + CH], state[:, d, hd, :],
                                        start=True, stop=True)
                            ins.then_inc(aux_full, 1)
                    for d in range(2) if kind == "vn" else ():
                        bank, n = aux("vn", i, d)
                        aux_open(n)
                        if i:
                            aux_freed(pe, AUX[("ks", i, d)])
                        for hd in range(4):
                            rhs = rr[:, d, hd, :] if i else vt[:, chunk[d], hd, :]
                            ins = M(bank[0:CH, P * hd:P * hd + P], (tm if d else um)[:, 2 * chunk[d] + d, hd, :], rhs,
                                    start=True, stop=True)
                        ins.then_inc(aux_full, 1)
                    for d in range(2) if kind == "od" else ():
                        bank, n = aux("od", i, d)
                        aux_open(n)
                        aux_freed(pe, AUX[("vn", i, d)])
                        unit = 2 * chunk[d] + d
                        for hd in range(4):
                            ins = M(bank[:, CH * hd:CH * hd + CH], vnew[:, d, hd, :], att[:, unit, hd, :], start=True, stop=i == 0)
                            if i:
                                ins = M(bank[:, CH * hd:CH * hd + CH], state[:, d, hd, :], eg[:, unit, hd, :], start=False, stop=True)
                        ins.then_inc(aux_full, 1)
                    if kind == "su":
                        for d in range(2):
                            bank, n = aux("su", i, d)
                            aux_open(n)
                            pe.wait_ge(vdec_ready, 2 * i + d + 1)
                            for hd in range(4):
                                ins = M(bank[:, P * hd:P * hd + P], kt[:, chunk[d], hd, :], vdec[:, d, hd, :], start=True, stop=True)
                            ins.then_inc(aux_full, 1)
                if kind == "delta_norm":
                    for e in range(2):
                        bank, n = aux("dstat", e)
                        aux_open(n)
                        pe.wait_ge(dsq_ready, 1)
                        for m in range(2):
                            ins = M(bank[:, ROWS * m:ROWS * m + ROWS], ones[:], dsq[:, 2 * e + m, :], start=True, stop=True)
                        ins.then_inc(aux_full, 1)
            for i in range(8):
                output(OUT2_O + i, OUT2_P + i, xh, xl, ROWS, each=(lambda kk: pe.wait_ge(mg_low, kk + 1)) if i == 0 else None)
            norm_stat(6)
            up_loop(UP2_O, UP2_P, ROWS, 7)
            down_loop(1, DOWN2_O, DOWN2_P, ROWS)
            norm_stat(8)


def pack(w, k_tiles):
    import numpy as np
    rows, cols = w.shape
    return np.ascontiguousarray(w.reshape(k_tiles, P, cols // P, P).transpose(2, 1, 0, 3).reshape(cols // P, P, k_tiles * P))


def columns(v, tiles):
    return v.reshape(-1, tiles, P).transpose(2, 0, 1).reshape(P, -1)


def constants():
    import numpy as np
    f = np.float32
    j, i = np.arange(P)[:, None], np.arange(P)[None, :]
    masks = np.zeros((P, 8, P), np.int32)
    masks[:, 0] = j == i
    for l in range(1, 8):
        b = 2 ** (l - 1)
        masks[:, l] = ((i // b) % 2 == 1) & (j // b == i // b - 1)
    d = np.arange(64)
    ang = 2 * np.pi * np.outer(d, d) / 64
    fmat = np.zeros((P, 2 * P), f)
    for g in range(2):
        fmat[64 * g:64 * g + 64, 64 * g:64 * g + 64] = np.cos(ang) / 8
        fmat[64 * g:64 * g + 64, P + 64 * g:P + 64 * g + 64] = np.sin(ang) / 8
    t = np.arange(LEN)
    ang = 2 * np.pi * ((t[:, None] * t[None, META:]) % LEN) / LEN
    cm = np.stack([np.cos(ang), -np.sin(ang)], 1) / np.sqrt(LEN)
    cmat = cm.reshape(NC, CH, 2, ROWS).transpose(1, 0, 2, 3).astype(f)
    a, b = np.arange(CH)[:, None], np.arange(CH)[None, :]
    tri = np.stack([a <= b, a >= b], 1).astype(f)
    lvl = np.stack([(a // SUB == b // SUB + 1) & ((a // SUB) % 2 == 1), (a >= 2 * SUB) & (b < 2 * SUB)], 1).astype(f)
    eye = np.broadcast_to(np.eye(SUB, dtype=f), (P, SUB, SUB))
    return {"masks": masks, "fmat": fmat, "cmat": cmat, "tri": tri, "lvl": lvl, "eye17": eye,
            "ident": np.eye(P, dtype=f), "ones": np.ones((P, P), f)}


def kernel(**inputs):
    import numpy as np
    import concourse.bacc as bacc
    from concourse.bass_utils import run_bass_kernel_spmd

    x = {n: np.asarray(v) for n, v in inputs.items()}
    for n in ("x", "mem"):
        x[n] = x[n][0]
    for n in list(x):
        if x[n].ndim > 1 and x[n].shape[0] == 1 and n not in ("x", "mem"):
            x[n] = x[n][0]

    w = x["w_in"]
    at = [0, 512, 1024, 2048, 2064, 2576, 3088, 3600, 4112, 6160]
    gq, gk, gv, glr, hq, hf, hi, xq, gate = (w[:, at[n]:at[n + 1]] for n in range(9))
    w2 = x["w_in_2"]
    at = [0, 512, 2048, 3584, 4096, 4112, 7184]
    fo, sc, qkv, z, ba, gates = (w2[:, at[n]:at[n + 1]] for n in range(6))
    sc = pack(sc, KT)
    gates = pack(gates, KT)

    def halves(w_):
        p = pack(w_, 4)
        return p.reshape(4, 2, P, 512).transpose(0, 2, 1, 3).reshape(4, P, 1024)

    def up(w_):
        p = pack(w_, KT)
        return np.stack([p[:FT], p[FT:]], 1).reshape(UP, P, 1024)

    by_step = {}
    for n, (name, width) in enumerate((("qkv", 12), ("z", 4), ("fourier_in", 4))):
        p = pack((qkv, z, fo)[n], KT)
        for i in range(width):
            by_step[(name, i)] = p[i]
    for i in range(4):
        for j in range(3):
            by_step[("sconv", i, j)] = sc[4 * j + i]
    for b in range(3):
        p = halves(x[("w_fourier_2", "w_sconv_out_2", "w_dn_out_2")[b]])
        for i in range(8):
            by_step[("gate", b, i)] = gates[8 * b + i]
            by_step[("branch", b, i)] = p[i // 2]
    mixer = [by_step[step] for step, (_, _, half) in MIX_OUT.items() if not half]
    w_out = pack(x["w_out"], 16).reshape(8, P, 2, 1024)
    w_out = np.stack([w_out[i, :, half] for i, half in W_OUT])
    panels = np.concatenate([pack(x["w_mem_kv"], KT)] + [pack(p, KT) for p in (hf, gk, gq, hq, xq, gate, gv, hi)]
                            + [w_out, up(x["ffn1_wi_2"]), np.stack(mixer), pack(x["w_out_2"], KT), up(x["ffn2_wi_2"])])
    down = np.concatenate([pack(x["ffn1_wo_2"], FT), pack(x["ffn2_wo_2"], FT)])

    def rows(m):
        return m.T.reshape(KT, P, -1).transpose(1, 0, 2)

    table = {"norm_w": columns(x["norm_w"], 8), "mem_norm": columns(x["mem_norm_w"], 8),
             "final": columns(x["final_norm_w"], 8), "gains": columns(x["norm_gains_2"], 8),
             "b_gate": columns(x["gla_b_gate"], 4), "gla_norm": columns(x["gla_norm_w"], 2),
             "lb": columns(x["hgrn_lower_bounds"], 4), "hgrn_norm": columns(x["hgrn_norm_w"], 1),
             "xattn_norm": columns(x["xattn_norm_w"], 1), "sconv": columns(x["sconv_w_2"], 4),
             "dconv": columns(x["dn_conv_w_2"], 12), "dn_norm": columns(x["dn_norm_2"], 1),
             "a_log": np.broadcast_to(x["dn_A_log_2"].reshape(1, 8), (P, 8)),
             "dt_bias": np.broadcast_to(x["dn_dt_bias_2"].reshape(1, 8), (P, 8))}
    arrays = {"panels": panels, "down": down, "x": rows(x["x"]), "mem": rows(x["mem"]), "meta": rows(x["meta_tokens_2"]),
              "vec": np.concatenate([table[n] for n in VEC_AT], 1), "upw": x["gla_w_gate_up"],
              "wglr": glr.reshape(KT, P, 16).transpose(1, 0, 2), "wba": ba.reshape(KT, P, 16).transpose(1, 0, 2),
              **constants()}
    arrays = {"in_" + n: np.ascontiguousarray(v) for n, v in arrays.items()}
    nc = bacc.Bacc("TRN2", target_bir_lowering=False, num_devices=1)
    a = {n[3:]: nc.dram_tensor(n, v.shape, mybir.dt.from_np(v.dtype), kind="ExternalInput").ap() for n, v in arrays.items()}
    a["out"] = nc.dram_tensor("out", (P, KT, ROWS), mybir.dt.float32, kind="ExternalOutput").ap()
    a["spill"] = nc.dram_tensor("spill", (P, KT, ROWS), mybir.dt.float32, kind="Internal").ap()
    for n in ("blocks", "inverses"):
        a[n] = nc.dram_tensor(n, (4, 32, SUB, SUB), mybir.dt.float32, kind="Internal").ap()
    build(nc, a)
    got = run_bass_kernel_spmd(nc, [arrays], core_ids=[0]).results[0]["out"]
    return np.ascontiguousarray(got.transpose(2, 1, 0).reshape(1, ROWS, KT * P))
```
